# Optimizing a Trainium2 kernel written in Bass

```python
import jax
import jax.numpy as jnp
from jax import lax
import numpy as np

D_MODEL = 1024
BATCH = 1
SEQ = 1024
DEPTH = 1
DEC_BATCH = 1
DEC_SEQ = 32
PAST_LEN = 2048

CHUNK = 64
N_META = 16
Q_BLOCK = 128
EPS = 1e-6
NEG = -1e30
MLA_HEADS = 8
QK_NOPE = 64
QK_ROPE = 32
V_DIM = 64
Q_LORA = 256
KV_LORA = 128
ROPE_BASE = 10000.0
ATTN_SCALE = (QK_NOPE + QK_ROPE) ** -0.5
MLA_DIM = MLA_HEADS * V_DIM
MLA_COLS = Q_LORA + KV_LORA + QK_ROPE
RWKV_HEADS = 8
RWKV_HEAD = 64
RWKV_DIM = RWKV_HEADS * RWKV_HEAD
DECAY_LORA = 64
AAA_LORA = 64
GATE_LORA = 128
LNX_EPS = 64e-5
RWKV_COLS = 3 * RWKV_DIM + DECAY_LORA + AAA_LORA + GATE_LORA
IN_COLS = MLA_COLS + RWKV_COLS
MIX_DIM = MLA_DIM + RWKV_DIM
D_FF = -(-8 * D_MODEL // (3 * 256)) * 256

kernel_name = 'hymba_mla_rwkv7_streaming_step'

def rmsnorm(x, g, eps=EPS):
    xf = x.astype(jnp.float32)
    y = xf * lax.rsqrt(jnp.mean(xf * xf, axis=-1, keepdims=True) + eps)
    return (y * g.astype(jnp.float32)).astype(x.dtype)

def rope(x, pos):
    half = x.shape[-1] // 2
    inv = ROPE_BASE ** (-jnp.arange(half, dtype=jnp.float32) / half)
    ang = pos.astype(jnp.float32)[:, None] * inv[None, :]
    shape = (ang.shape[0],) + (1,) * (x.ndim - 3) + (half,)
    cos = jnp.cos(ang).reshape(shape).astype(x.dtype)
    sin = jnp.sin(ang).reshape(shape).astype(x.dtype)
    x1, x2 = x[..., :half], x[..., half:]
    return jnp.concatenate([x1 * cos - x2 * sin, x1 * sin + x2 * cos], axis=-1)

def mla_kv_rows(p_mla, pos, kv_norm_g, kn_rope_g):
    c = rmsnorm(p_mla[..., Q_LORA:Q_LORA + KV_LORA], kv_norm_g)
    kr = rope(rmsnorm(p_mla[..., Q_LORA + KV_LORA:MLA_COLS], kn_rope_g), pos)
    return c, kr

def mla_queries(p_mla, pos, q_norm_g, w_q_up, qn_nope_g, qn_rope_g):
    b, l = p_mla.shape[:2]
    ql = rmsnorm(p_mla[..., :Q_LORA], q_norm_g)
    q = (ql @ w_q_up).reshape(b, l, MLA_HEADS, QK_NOPE + QK_ROPE)
    qn = rmsnorm(q[..., :QK_NOPE], qn_nope_g)
    qr = rope(rmsnorm(q[..., QK_NOPE:], qn_rope_g), pos)
    return qn, qr

def expand_latent(c, w_kv_up, kn_nope_g):
    b, l = c.shape[:2]
    kv = (c @ w_kv_up).reshape(b, l, MLA_HEADS, QK_NOPE + V_DIM)
    return rmsnorm(kv[..., :QK_NOPE], kn_nope_g), kv[..., QK_NOPE:]

def attend_block(qn, qr, q_chunk, kn, kr, v, k_chunk):
    s = jnp.einsum('bqhd,bkhd->bhqk', qn, kn) + jnp.einsum('bqhr,bkr->bhqk', qr, kr)
    s = s.astype(jnp.float32) * ATTN_SCALE
    mask = k_chunk[None, :] <= q_chunk[:, None]
    s = jnp.where(mask[None, None], s, NEG)
    p = jax.nn.softmax(s, axis=-1).astype(v.dtype)
    return jnp.einsum('bhqk,bkhd->bqhd', p, v)

def prompt_attention(qn, qr, q_chunk, kn, kr, v, k_chunk):
    b, s = qn.shape[:2]
    nb = s // Q_BLOCK

    def blocks(t):
        return jnp.swapaxes(t.reshape((b, nb, Q_BLOCK) + t.shape[2:]), 0, 1)

    out = lax.map(lambda a: attend_block(a[0], a[1], a[2], kn, kr, v, k_chunk),
                  (blocks(qn), blocks(qr), q_chunk.reshape(nb, Q_BLOCK)))
    return jnp.swapaxes(out, 0, 1).reshape(b, s, MLA_DIM)

def heads(t):
    return t.reshape(t.shape[:-1] + (RWKV_HEADS, RWKV_HEAD))

def rwkv_inputs(p_rw, prev, mu_shift, w0, w2, a0, a2, k_k, k_a):
    shifted = jnp.concatenate([prev[:, None, :].astype(p_rw.dtype), p_rw[:, :-1]], axis=1)
    xm = p_rw + (shifted - p_rw) * mu_shift
    o = RWKV_DIM
    r, k, v = xm[..., :o], xm[..., o:2 * o], xm[..., 2 * o:3 * o]
    wl = xm[..., 3 * o:3 * o + DECAY_LORA]
    al = xm[..., 3 * o + DECAY_LORA:3 * o + DECAY_LORA + AAA_LORA]
    gl = xm[..., 3 * o + DECAY_LORA + AAA_LORA:]
    w_log = -jax.nn.softplus(-(w0 + jnp.tanh(wl) @ w2).astype(jnp.float32)) - 0.5
    decay = jnp.exp(-jnp.exp(w_log))
    a = jax.nn.sigmoid((a0 + al @ a2).astype(jnp.float32))
    kk = heads((k * k_k).astype(jnp.float32))
    kk = kk / jnp.maximum(jnp.sqrt(jnp.sum(kk * kk, axis=-1, keepdims=True)), 1e-12)
    k_eff = k.astype(jnp.float32) * (1.0 + (a - 1.0) * k_a.astype(jnp.float32))
    return (heads(r.astype(jnp.float32)), heads(decay), heads(k_eff),
            heads(v.astype(jnp.float32)), kk, heads(a), gl)

def wkv_scan(s0, r, w, k, v, kk, a):
    def step(S, inp):
        r_t, w_t, k_t, v_t, kk_t, a_t = inp
        sa = jnp.einsum('bhvk,bhk->bhv', S, -kk_t)
        S = (S * w_t[:, :, None, :] + sa[..., None] * (kk_t * a_t)[:, :, None, :]
             + v_t[..., None] * k_t[:, :, None, :])
        return S, jnp.einsum('bhvk,bhk->bhv', S, r_t)

    xs = tuple(jnp.swapaxes(t, 0, 1) for t in (r, w, k, v, kk, a))
    S, ys = lax.scan(step, s0.astype(jnp.float32), xs)
    return S, jnp.swapaxes(ys, 0, 1)

def rwkv_out(y, r, k, v, gl, g2, r_k, lnx_g, lnx_b):
    b, l = y.shape[:2]
    mean = jnp.mean(y, axis=-1, keepdims=True)
    var = jnp.mean(jnp.square(y - mean), axis=-1, keepdims=True)
    yn = ((y - mean) * lax.rsqrt(var + LNX_EPS)).reshape(b, l, RWKV_DIM)
    yn = yn * lnx_g.astype(jnp.float32) + lnx_b.astype(jnp.float32)
    bonus = (jnp.sum(r * k * r_k.astype(jnp.float32), axis=-1, keepdims=True) * v).reshape(b, l, RWKV_DIM)
    g = jax.nn.sigmoid(gl) @ g2
    return (yn + bonus).astype(gl.dtype) * g

def layer_tail(x, attn, rw, attn_out_g, w_out, norm_ffn_g, w_gate, w_up, w_down):
    mix = jnp.concatenate([rmsnorm(attn, attn_out_g), rw], axis=-1)
    h = x + mix @ w_out
    u = rmsnorm(h, norm_ffn_g)
    return h + (jax.nn.silu(u @ w_gate) * (u @ w_up)) @ w_down

def setup_inputs(seed: int = 0) -> dict:
    key = jax.random.key(seed)
    ks = jax.random.split(key, 40)

    def nrm(k, shape, scale):
        return jax.random.normal(k, shape, jnp.float32) * scale

    return {
        'x_prompt': nrm(ks[0], (BATCH, SEQ, D_MODEL), 1.0),
        'x_sample': nrm(ks[1], (DEC_BATCH, DEC_SEQ, D_MODEL), 1.0),
        'cache_kv_latent': nrm(ks[2], (DEC_BATCH, PAST_LEN, KV_LORA), 1.0),
        'cache_k_rope': nrm(ks[3], (DEC_BATCH, PAST_LEN, QK_ROPE), 1.0),
        'state_wkv': nrm(ks[4], (DEC_BATCH, RWKV_HEADS, RWKV_HEAD, RWKV_HEAD), 0.1),
        'state_shift': nrm(ks[5], (DEC_BATCH, RWKV_COLS), 1.0),
        'meta_tokens': nrm(ks[6], (N_META, D_MODEL), 1.0),
        'norm_mix_g': 1.0 + nrm(ks[7], (D_MODEL,), 0.02),
        'w_in': nrm(ks[8], (D_MODEL, IN_COLS), D_MODEL ** -0.5),
        'q_norm_g': 1.0 + nrm(ks[9], (Q_LORA,), 0.02),
        'w_q_up': nrm(ks[10], (Q_LORA, MLA_HEADS * (QK_NOPE + QK_ROPE)), Q_LORA ** -0.5),
        'kv_norm_g': 1.0 + nrm(ks[11], (KV_LORA,), 0.02),
        'w_kv_up': nrm(ks[12], (KV_LORA, MLA_HEADS * (QK_NOPE + V_DIM)), KV_LORA ** -0.5),
        'qn_nope_g': 1.0 + nrm(ks[13], (QK_NOPE,), 0.02),
        'qn_rope_g': 1.0 + nrm(ks[14], (QK_ROPE,), 0.02),
        'kn_nope_g': 1.0 + nrm(ks[15], (QK_NOPE,), 0.02),
        'kn_rope_g': 1.0 + nrm(ks[16], (QK_ROPE,), 0.02),
        'attn_out_g': 1.0 + nrm(ks[17], (MLA_DIM,), 0.02),
        'mu_shift': jax.random.uniform(ks[18], (RWKV_COLS,), jnp.float32, 0.0, 1.0),
        'w0': jax.random.uniform(ks[19], (RWKV_DIM,), jnp.float32, -6.0, -1.0),
        'w2': nrm(ks[20], (DECAY_LORA, RWKV_DIM), 0.1 * DECAY_LORA ** -0.5),
        'a0': nrm(ks[21], (RWKV_DIM,), 0.1),
        'a2': nrm(ks[22], (AAA_LORA, RWKV_DIM), 0.5 * AAA_LORA ** -0.5),
        'g2': nrm(ks[23], (GATE_LORA, RWKV_DIM), GATE_LORA ** -0.5),
        'k_k': 0.85 + nrm(ks[24], (RWKV_DIM,), 0.02),
        'k_a': 1.0 + nrm(ks[25], (RWKV_DIM,), 0.02),
        'r_k': nrm(ks[26], (RWKV_HEADS, RWKV_HEAD), 0.1),
        'lnx_g': 1.0 + nrm(ks[27], (RWKV_DIM,), 0.02),
        'lnx_b': nrm(ks[28], (RWKV_DIM,), 0.02),
        'w_out': nrm(ks[29], (MIX_DIM, D_MODEL), MIX_DIM ** -0.5),
        'norm_ffn_g': 1.0 + nrm(ks[30], (D_MODEL,), 0.02),
        'w_gate': nrm(ks[31], (D_MODEL, D_FF), D_MODEL ** -0.5),
        'w_up': nrm(ks[32], (D_MODEL, D_FF), D_MODEL ** -0.5),
        'w_down': nrm(ks[33], (D_FF, D_MODEL), D_FF ** -0.5),
    }

def reference(x_prompt, x_sample, cache_kv_latent, cache_k_rope, state_wkv, state_shift,
              meta_tokens, norm_mix_g, w_in, q_norm_g, w_q_up, kv_norm_g, w_kv_up,
              qn_nope_g, qn_rope_g, kn_nope_g, kn_rope_g, attn_out_g, mu_shift, w0, w2,
              a0, a2, g2, k_k, k_a, r_k, lnx_g, lnx_b, w_out, norm_ffn_g, w_gate, w_up, w_down):
    b, s = x_prompt.shape[:2]
    L = N_META + s
    xf = jnp.concatenate([jnp.broadcast_to(meta_tokens.astype(x_prompt.dtype)[None], (b, N_META, D_MODEL)),
                          x_prompt], axis=1)
    proj = rmsnorm(xf, norm_mix_g) @ w_in
    p_mla, p_rw = proj[..., :MLA_COLS], proj[..., MLA_COLS:]
    pos = jnp.arange(L, dtype=jnp.int32)
    k_chunk = jnp.concatenate([jnp.full((N_META,), -1, jnp.int32),
                               jnp.arange(s, dtype=jnp.int32) // CHUNK])
    q_chunk = jnp.arange(s, dtype=jnp.int32) // CHUNK
    c_p, kr_p = mla_kv_rows(p_mla, pos, kv_norm_g, kn_rope_g)
    kn_p, v_p = expand_latent(c_p, w_kv_up, kn_nope_g)
    qn_p, qr_p = mla_queries(p_mla[:, N_META:], pos[N_META:], q_norm_g, w_q_up, qn_nope_g, qn_rope_g)
    attn_p = prompt_attention(qn_p, qr_p, q_chunk, kn_p, kr_p, v_p, k_chunk)
    r, w, k, v, kk, a, gl = rwkv_inputs(p_rw, jnp.zeros((b, RWKV_COLS), p_rw.dtype),
                                        mu_shift, w0, w2, a0, a2, k_k, k_a)
    wkv_p, y_rw = wkv_scan(jnp.zeros((b, RWKV_HEADS, RWKV_HEAD, RWKV_HEAD), jnp.float32),
                           r, w, k, v, kk, a)
    rw_p = rwkv_out(y_rw[:, N_META:], r[:, N_META:], k[:, N_META:], v[:, N_META:],
                    gl[:, N_META:], g2, r_k, lnx_g, lnx_b)
    y_prompt = layer_tail(x_prompt, attn_p, rw_p, attn_out_g, w_out, norm_ffn_g, w_gate, w_up, w_down)
    shift_p = p_rw[:, -1]

    db, ds = x_sample.shape[:2]
    past = cache_kv_latent.shape[1]
    proj_s = rmsnorm(x_sample, norm_mix_g) @ w_in
    ps_mla, ps_rw = proj_s[..., :MLA_COLS], proj_s[..., MLA_COLS:]
    pos_s = past + jnp.arange(ds, dtype=jnp.int32)
    c_s, kr_s = mla_kv_rows(ps_mla, pos_s, kv_norm_g, kn_rope_g)
    c_all = jnp.concatenate([cache_kv_latent.astype(c_s.dtype), c_s], axis=1)
    kr_all = jnp.concatenate([cache_k_rope.astype(kr_s.dtype), kr_s], axis=1)
    kn_s, v_s = expand_latent(c_all, w_kv_up, kn_nope_g)
    qn_s, qr_s = mla_queries(ps_mla, pos_s, q_norm_g, w_q_up, qn_nope_g, qn_rope_g)
    k_chunk_s = jnp.arange(past + ds, dtype=jnp.int32) // CHUNK
    attn_s = attend_block(qn_s, qr_s, pos_s // CHUNK, kn_s, kr_all, v_s, k_chunk_s).reshape(db, ds, MLA_DIM)
    r2, w2_, k2, v2, kk2, a2_, gl2 = rwkv_inputs(ps_rw, state_shift, mu_shift, w0, w2, a0, a2, k_k, k_a)
    wkv_s, y_rw_s = wkv_scan(state_wkv, r2, w2_, k2, v2, kk2, a2_)
    rw_s = rwkv_out(y_rw_s, r2, k2, v2, gl2, g2, r_k, lnx_g, lnx_b)
    y_sample = layer_tail(x_sample, attn_s, rw_s, attn_out_g, w_out, norm_ffn_g, w_gate, w_up, w_down)
    shift_s = ps_rw[:, -1].astype(state_shift.dtype)

    return (y_prompt, y_sample, c_p, kr_p, wkv_p.astype(x_prompt.dtype), shift_p,
            c_s, kr_s, wkv_s.astype(state_wkv.dtype), shift_s)


_drawn_inputs = setup_inputs


def setup_inputs(seed=0):
    import zlib

    import numpy as np

    out = dict(_drawn_inputs(seed))
    spreads = {}
    factors = {'q_norm_g': 4.565,
     'qn_nope_g': 4.872,
     'qn_rope_g': 8.0,
     'kn_nope_g': 5.227,
     'attn_out_g': 4.895,
     'w2': 8.0,
     'lnx_g': 8.0,
     'lnx_b': 8.0,
     'norm_ffn_g': 4.499}
    for name, (base, spread) in spreads.items():
        noise = np.random.default_rng([zlib.crc32(name.encode()), seed]).standard_normal(out[name].shape)
        drawn = base * np.exp(spread * noise) if base else spread * noise
        out[name] = jnp.asarray(drawn.astype(out[name].dtype))
    for name, factor in factors.items():
        out[name] = (out[name] * factor).astype(out[name].dtype)
    return out
```

```python
import numpy as np
from contextlib import ExitStack
import concourse.bass as bass
from concourse import mybir

F32 = mybir.dt.float32
ALU = mybir.AluOpType
ACT = mybir.ActivationFunctionType
AX = mybir.AxisListType

P = 128
D = 1024
KD = D // P
SEQ, META, SAMPLE, PAST = 1024, 16, 32, 2048
CHUNK = 64
TILES = SEQ // P + 1
SAMPLE_ROW = CHUNK
H = 8
NOPE, ROPE, VD = 64, 32, 64
QKD = NOPE + ROPE
QL, KVL = 256, 128
MLA = QL + KVL + ROPE
RW = 512
LORA = 64
GATE = 128
RCOLS = 3 * RW + 2 * LORA + GATE
COLS = MLA + RCOLS
IPC = 6
IPW = COLS // IPC
KEYS = META + SEQ
TOK = SEQ + SAMPLE
TN = TOK // 3
MLA_OUT = H * VD
FF = 2816
FB = FF // P
EPS = 1e-6
LNX_EPS = 64e-5
DECAY = float(np.exp(np.float64(-0.5)))
ATTN_SCALE = float(QKD) ** -0.5
NEG = -1e30
LEVELS = (2, 4, 8, 16, 32)
ACT_STEPS, POOL_STEPS, DVE_STEPS = 10, 3, 40

VEC = {}
_at = 0
for _n, _w in (("q_norm_g", QL), ("kv_norm_g", KVL), ("kn_rope_g", ROPE), ("qn_nope_g", NOPE), ("qn_rope_g", ROPE),
               ("kn_nope_g", NOPE), ("mu_shift", RCOLS), ("w0", RW), ("a0", RW), ("k_k", RW), ("k_a", RW),
               ("r_k", RW), ("lnx_g", RW), ("lnx_b", RW)):
    VEC[_n] = (_at, _w)
    _at += _w
VECS = _at

CON = {}
_at = 0
for _n, _w in (("ident", P), ("one", 1), ("cum_inc", P), ("cum_exc", P), ("chunk", 2), ("b_mask", 2 * CHUNK),
               ("k_mask", 2 * CHUNK), ("eye", CHUNK), ("first", CHUNK), ("own", 2), ("levels", len(LEVELS) * CHUNK), ("live", 1),
               ("inv3", 3), ("inv24", 24), ("minus_half", 24), ("rope", TILES * 4 * ROPE // 2)):
    CON[_n] = (_at, _w)
    _at += _w
CONS = _at


def constants():
    c = np.zeros((P, CONS), np.float32)

    def put(name, value):
        a, w = CON[name]
        c[:, a:a + w] = np.asarray(value, np.float32).reshape(P, w)

    row = np.arange(P)
    same = row[:, None] // CHUNK == row[None, :] // CHUNK
    put("ident", np.eye(P))
    put("one", np.ones((P, 1)))
    put("cum_inc", np.where(same & (row[:, None] <= row[None, :]), -DECAY, 0.0))
    put("cum_exc", np.where(same & (row[:, None] < row[None, :]), -DECAY, 0.0))
    put("chunk", np.where(row[:, None] // CHUNK == np.arange(2)[None, :], -DECAY, 0.0))
    i, t = (row % CHUNK)[:, None], np.arange(CHUNK)[None, :]
    pair = (i % 2 == 0) & (t == i + 1)
    put("b_mask", np.concatenate([pair, i <= t], 1))
    put("k_mask", np.concatenate([i < t, i <= t], 1))
    put("eye", i == t)
    put("own", row[:, None] // CHUNK == np.arange(2)[None, :])
    put("first", (i % 2 == 1) & (t == i - 1))
    put("levels", np.concatenate([(i // s % 2 == 1) & (t // s == i // s - 1) for s in LEVELS], 1))
    put("live", (row < META) | ((row >= SAMPLE_ROW) & (row < SAMPLE_ROW + SAMPLE)))
    put("inv3", np.broadcast_to([1 / QL, 1 / KVL, 1 / ROPE], (P, 3)))
    put("inv24", np.broadcast_to([1 / NOPE] * 16 + [1 / ROPE] * 8, (P, 24)))
    put("minus_half", np.full((P, 24), -0.5))
    half = ROPE // 2
    inv = np.float32(10000.0) ** (-np.arange(half, dtype=np.float32) / np.float32(half))
    pos = np.zeros((TILES, P), np.float32)
    pos[0, :META] = np.arange(META)
    pos[0, SAMPLE_ROW:SAMPLE_ROW + SAMPLE] = PAST + np.arange(SAMPLE)
    pos[1:] = (META + np.arange(SEQ)).reshape(TILES - 1, P)
    ang = pos.T[:, :, None] * inv[None, None, :]
    cos, sin = np.cos(ang), np.sin(ang)
    put("rope", np.concatenate([cos, cos, sin, -sin], 2).reshape(P, -1))
    return c


def bcast(ap, axis, n):
    shape = list(ap.shape)
    shape.insert(axis, n)
    return ap.unsqueeze(axis).broadcast_to(shape)


def is_first(t):
    return type(t) is int and t == 0


def wait(e, sem, value):
    if type(value) is int and value <= 0:
        return
    e.wait_ge(sem, value)


class Chain:

    def __init__(self, engine, sem, per_tile):
        self.e, self.sem, self.per_tile, self.t, self.n = engine, sem, per_tile, 0, 0

    def tile(self, t):
        if self.n and self.n != self.per_tile:
            raise ValueError(f"{self.sem} counts {self.n} a tile, not {self.per_tile}")
        self.t, self.n = t, 0

    def __call__(self, ins):
        self.n += 1
        ins.then_inc(self.sem, 1)
        self.e.wait_ge(self.sem, self.t * self.per_tile + self.n)


def layer_inputs(nc, g, io, phase):
    sb, sem = phase.sb, g.sem
    pb = g.pb
    win = sb("win", [P, KD, COLS])
    xt = [sb(f"xt{i}", [P, KD, P]) for i in range(2)]
    xsq = sb("xsq", [P, KD, P])
    proj = [sb(f"proj{i}", [P, COLS]) for i in range(2)]
    mixed = [sb(f"mixed{i}", [P, RCOLS]) for i in range(2)]
    wq = sb("wq", [P, QL // P, H * QKD])
    wkv = g.wkv
    vec = sb("vec", [P, VECS])
    w2a2 = sb("w2a2", [P, RW])
    g2 = sb("g2", [P, RW])
    rstd = [sb(f"rstd{i}", [P, 1]) for i in range(2)]
    mean_sq = sb("mean_sq", [P, 1])
    con = g.con
    gmix = sb("gmix", [P, KD])

    lat = sb("lat", [P, QL + KVL])
    st3 = sb("st3", [P, 3])
    krn = sb("krn", [P, 3, ROPE])
    kr = sb("kr", [P, ROPE])
    st24 = sb("st24", [P, 24])
    n8 = sb("n8", [P, 8])
    b8 = sb("b8", [P, 8])
    y8 = sb("y8", [P, 8])
    v8 = sb("v8", [P, 8])
    g_qk = sb("g_qk", [P, NOPE])
    loraT = sb("loraT", [P, 2 * P])
    sig = sb("sig", [P, RW])
    aB = sb("aB", [P, RW])
    kk = sb("kk", [P, RW])
    keff = sb("keff", [P, RW])
    rR = sb("rR", [P, RW])
    kK = sb("kK", [P, RW])
    aA = sb("aA", [P, RW])
    tmp = sb("tmp", [P, RW])
    pc = sb("pc", [P, 8])
    area = sb("area", [P, 4992])
    k96 = area[:, 0:768].rearrange("p (h d) -> p h d", h=H)
    q96 = area[:, 768:1536].rearrange("p (h d) -> p h d", h=H)
    sqk = area[:, 1536:2048].rearrange("p (h d) -> p h d", h=H)
    sqq = area[:, 2048:2816].rearrange("p (h d) -> p h d", h=H)
    rope2 = area[:, 1536:2048].rearrange("p (a h d) -> p a h d", a=2, h=H)
    kts = area[0:QKD, 2816:3840].rearrange("p (h n) -> p h n", h=H)
    qts = area[0:QKD, 1536:2560].rearrange("p (h n) -> p h n", h=H)
    vst = area[:, 3840:4352].rearrange("p (h n) -> p h n", h=H)
    junk = area[:, 3840:4096]
    lw = area[:, 4352:4480]
    sg = area[:, 4480:4608]
    latT = area[:, 4608:4992]
    XT = area[:, 0:2048].rearrange("p (j a n) -> p j a n", j=4, a=4)
    GK = area[:, 2048:3072].rearrange("p (h n) -> p h n", h=H)
    GB = area[:, 3072:3584].rearrange("p (h n) -> p h n", h=H)
    Lraw = area[:, 3584:4096].rearrange("p (h n) -> p h n", h=H)
    Em = area[:, 4096:4608].rearrange("p (h n) -> p h n", h=H)
    SA = area[:, 3584:4096]
    Ls = [x[:, :].rearrange("p (h n) -> p h n", h=H) for x in (keff, aA)]
    Dm = rR[:, :].rearrange("p (h n) -> p h n", h=H)
    U = tmp
    yb = sb("yb", [P, RW])
    T1h = yb[:, :].rearrange("p (h n) -> p h n", h=H)
    rwT = sb("rwT", [P, 4, P])
    pcm = sb("pcm", [P, 2, 4, 2])
    SP_ = sb("state_p", [P, 4, P])
    SS_ = sb("state_s", [P, 4, P])

    def v_(name):
        a, w = VEC[name]
        return vec[:, a:a + w]

    def c_(name, rows=slice(0, P)):
        a, w = CON[name]
        return con[rows, a:a + w]

    ident = c_("ident")
    heads = lambda ap: ap.rearrange("p (h n) -> p h n", h=H)
    half = ROPE // 2

    names = """x_in0 x_in1 s_loaded x_scaled x_squared ssq_ps rstd_ok ip_ps p_ok sh_in lat_ssq lat_ok kr_ok latT_ps latT_ok
        up_ps sqk_ok sqq_ok v_ok k96_ok q96_ok kT_ps qT_ps kts_ok qts_ok xm_ok lw_ok sg_e sg_ok loraT_ps loraT_ok lora_ps
        z_ok z_e sig_ok a_ok_z a_e a_ok cum_ps rR_e kK_e aA_e pc_ok kkr_ok kksq_ok kk_ok kka_ok keff_ok
        R_ok K_ok A_ok B_ok rk_ok bon_ok bonv_ok XT_ps XT_act XT_dve G_ps gmask_ok Lraw_ok Ls_ok T1_ps T1_ok ED_ps E_ok D_ok
        U_ps U_ok SA_ps SA_ok dS_ps S_ok Y_ps gate_ps yc_ok ysq_ok rw_ok rwT_ps rwT_ok
        st_lat st_kv st_rw st_end init_ok mask_ok pe_waited sp_waited mean_ok st3_ms st3_ok st24_ms st24_ok n8_ms n8_ok v8_ms v8_ok dve_chain act_chain pool_chain dve_once act_once pool_once""".split()
    s = {n: sem(n) for n in names}
    w_piece = [sem(f"w_piece{n}") for n in range(IPC)]

    tab = lambda t: con[:, CON["rope"][0]:][:, bass.ds(t * 2 * ROPE, 2 * ROPE)] if type(t) is not int else \
        con[:, CON["rope"][0] + t * 2 * ROPE:CON["rope"][0] + (t + 1) * 2 * ROPE]

    def tiles(e, step):
        step(0, 0, 0)
        with e.Fori(0, (TILES - 3) // 2) as i:
            step(i * 2 + 1, 1, i)
            step(i * 2 + 2, 0, i + 1)
        step(TILES - 2, 1, (TILES - 2) // 2)
        step(TILES - 1, 0, (TILES - 1) // 2)

    def is_last(t, n=1):
        return type(t) is int and t + n > TILES - 1

    block = phase.block()

    @block.sync
    def _(sp):
        sp.dma_start(xt[0][:, :, :], io.x_tiles[0]).then_inc(s["x_in0"], 16)
        sp.dma_start(gmix[:, :], io.g_mix).then_inc(s["s_loaded"], 16)
        sp.dma_start(con[:, :], io.con).then_inc(s["s_loaded"], 16)
        for n in range(IPC):
            sp.dma_start(win[:, :, n * IPW:(n + 1) * IPW], io.w_in[n]).then_inc(w_piece[n], 16)
        sp.dma_start(xt[1][:, :, :], io.x_tiles[1]).then_inc(s["x_in1"], 16)
        for dst, src in ((vec[:, :], io.vec.partition_broadcast(P)), (wq[:, :, :], io.w_q_up), (wkv[:, :], io.w_kv_up),
                         (w2a2[:, :], io.w2a2), (g2[:, :], io.g2), (SS_[:, :, :], io.state_wkv)):
            sp.dma_start(dst, src).then_inc(s["s_loaded"], 16)

        def apart():
            sp.nop().then_inc(s["sp_waited"], 1)

        def store_rw(t):
            wait(sp, s["rwT_ok"], t + 1)
            apart()
            sp.dma_start(io.rwT[:, :, bass.ds(t * P, P)], rwT[:, :, :]).then_inc(s["st_rw"], 16)

        def step(t, b, u):
            wait(sp, s["p_ok"], t * IPC + IPC)
            apart()
            pr, sh = proj[b][:, MLA:], mixed[b]
            if is_first(t):
                sp.wait_ge(s["init_ok"], 1)
                sp.dma_start(proj[b][P - 1:P, MLA:], proj[b][META - 1:META, MLA:]).then_inc(s["sh_in"], 16)
                sp.dma_start(sh[1:CHUNK, :], pr[0:CHUNK - 1, :]).then_inc(s["sh_in"], 16)
                sp.dma_start(sh[CHUNK + 1:, :], pr[CHUNK:P - 1, :]).then_inc(s["sh_in"], 16)
                sp.dma_start(sh[CHUNK:CHUNK + 1, :], io.state_shift).then_inc(s["sh_in"], 16)
                sp.dma_start(io.shift_s, pr[SAMPLE_ROW + SAMPLE - 1:SAMPLE_ROW + SAMPLE, :]).then_inc(s["sh_in"], 16)
            else:
                wait(sp, s["bonv_ok"], t)
                wait(sp, s["dS_ps"], t * 2 - 1)
                wait(sp, s["Y_ps"], t * 2 - 1)
                wait(sp, s["sh_in"], t * 32 + 48)
                apart()
                sp.dma_start(sh[1:, :], pr[0:P - 1, :]).then_inc(s["sh_in"], 16)
                sp.dma_start(sh[0:1, :], proj[1 - b][P - 1:P, MLA:]).then_inc(s["sh_in"], 16)
            if not is_last(t, 2):
                sp.dma_start(xt[b][:, :, :], io.x_tiles[bass.ds(t + 2, 1)].rearrange("a p k n -> (a p) k n")
                             ).then_inc(s[f"x_in{b}"], 16)
            wait(sp, s["kr_ok"], t + 1)
            apart()
            if is_first(t):
                sp.dma_start(io.c_p[0:META, :], lat[0:META, QL:]).then_inc(s["st_lat"], 16)
                sp.dma_start(io.kr_p[0:META, :], kr[0:META, :]).then_inc(s["st_lat"], 16)
                sp.dma_start(io.c_s, lat[SAMPLE_ROW:SAMPLE_ROW + SAMPLE, QL:]).then_inc(s["st_lat"], 16)
                sp.dma_start(io.kr_s, kr[SAMPLE_ROW:SAMPLE_ROW + SAMPLE, :]).then_inc(s["st_lat"], 16)
            else:
                sp.dma_start(io.c_p[bass.ds(t * P + (META - P), P), :], lat[:, QL:]).then_inc(s["st_lat"], 16)
                sp.dma_start(io.kr_p[bass.ds(t * P + (META - P), P), :], kr[:, :]).then_inc(s["st_lat"], 16)
                store_rw(t - 1)
            wait(sp, s["kts_ok"], t + 1)
            wait(sp, s["qts_ok"], t + 1)
            wait(sp, s["v_ok"], t + 1)
            apart()
            if is_first(t):
                sp.dma_start(io.kT[:, :, 0:META], kts[:, :, 0:META]).then_inc(s["st_kv"], 16)
                sp.dma_start(io.v[0, 0:META], vst[0:META]).then_inc(s["st_kv"], 16)
                sp.dma_start(g.v_new[:, :, :], vst[SAMPLE_ROW:SAMPLE_ROW + SAMPLE]).then_inc(s["st_kv"], 16)
            else:
                sp.dma_start(io.kT[:, :, bass.ds(t * P + (META - P), P)], kts).then_inc(s["st_kv"], 16)
                sp.dma_start(io.qT[:, :, bass.ds(t * P - P, P)], qts).then_inc(s["st_kv"], 16)
                sp.dma_start(io.v[bass.ds(t, 1)].rearrange("a p h n -> (a p) h n"), vst).then_inc(s["st_kv"], 16)

        tiles(sp, step)
        last = TILES - 1
        sp.dma_start(io.shift_p, proj[last % 2][P - 1:P, MLA:]).then_inc(s["st_end"], 16)
        sp.wait_ge(s["S_ok"], 2 * TILES)
        for out, S in ((io.wkv_s, SS_), (io.wkv_p, SP_)):
            for a in range(2):
                r = slice(64 * a, 64 * a + 64)
                sp.dma_start(out[r], S[r, :, r]).then_inc(s["st_end"], 16)
        store_rw(last)
        sp.wait_ge(s["st_end"], 16 * 5)
        sp.wait_ge(s["st_lat"], 32 * TILES + 32)
        sp.wait_ge(s["st_kv"], 48 * TILES)
        sp.wait_ge(s["st_rw"], 16 * TILES)

    @block.tensor
    def _(pe):
        def apart():
            pe.nop().then_inc(s["pe_waited"], 1)

        def mm(out, lhsT, rhs, start=True, stop=True):
            return pe.matmul(out, lhsT, rhs, start=start, stop=stop)

        def fill(t, b, u):
            n, part = u // 2, u % 2
            if u == 0:
                wait(pe, s["x_scaled"], t + 1)
            if part == 0:
                wait(pe, s["p_ok"], t * IPC + n - 1)
                if n == 1:
                    wait(pe, s["mean_ok"], t + 1)
                if is_first(t):
                    pe.wait_ge(w_piece[n], 16)
            for k in range(4 * part, 4 * part + 4):
                last = mm(pb[n % 2][:, 0:IPW], xt[b][:, k, :], win[:, k, n * IPW:(n + 1) * IPW], k == 0, k == KD - 1)
            if part:
                last.then_inc(s["ip_ps"], 1)

        def ssq(t):
            wait(pe, s["x_squared"], t + 1)
            wait(pe, s["p_ok"], t * IPC)
            for k in range(KD):
                last = mm(pb[1][:, 400:401], xsq[:, k, :], c_("one"), k == 0, k == KD - 1)
            last.then_inc(s["ssq_ps"], 1)

        def rw_transposes(t):
            wait(pe, s["rw_ok"], t + 1)
            for j in range(4):
                last = pe.transpose(pb[5][:, j * P:(j + 1) * P], yb[:, j * P:(j + 1) * P], ident)
            last.then_inc(s["rwT_ps"], 1)

        def step(t, b, u):
            def f(u):
                if not is_last(t):
                    fill(t + 1, 1 - b, u)

            f(0)
            if not is_last(t):
                ssq(t + 1)
            f(1)
            wait(pe, s["lat_ok"], t + 1)
            for j in range(3):
                last = pe.transpose(pb[2][:, j * P:(j + 1) * P], lat[:, j * P:(j + 1) * P], ident)
            last.then_inc(s["latT_ps"], 1)
            if not is_first(t):
                rw_transposes(t - 1)
            f(2)
            wait(pe, s["latT_ok"], t + 1)
            wait(pe, s["rw_ok"], t)
            wait(pe, s["rwT_ok"], t)
            for i in range(2):
                mm(pb[3 + i][:, :], latT[:, QL:QL + P], wkv[:, 512 * i:512 * (i + 1)])
            for i in range(2):
                for k in range(2):
                    last = mm(pb[5 + i][:, 0:384], latT[:, k * P:(k + 1) * P], wq[:, k, 384 * i:384 * (i + 1)], k == 0, k == 1)
            last.then_inc(s["up_ps"], 1)
            f(3)
            wait(pe, s["lw_ok"], t + 1)
            wait(pe, s["sg_ok"], t + 1)
            pe.transpose(pb[7][:, 0:P], lw, ident)
            pe.transpose(pb[7][:, P:2 * P], sg[:, :], ident).then_inc(s["loraT_ps"], 1)
            wait(pe, s["loraT_ok"], t + 1)
            mm(pb[2][:, :], loraT[0:LORA, 0:P], w2a2[0:LORA, :])
            mm(pb[7][:, :], loraT[LORA:P, 0:P], w2a2[LORA:P, :]).then_inc(s["lora_ps"], 1)
            f(4)
            wait(pe, s["k96_ok"], t + 1)
            wait(pe, s["v_ok"], t + 1)
            for h in range(H):
                last = pe.transpose(pb[3 + h // 4][0:QKD, h % 4 * P:(h % 4 + 1) * P], k96[:, h, :], ident)
            last.then_inc(s["kT_ps"], 1)
            wait(pe, s["q96_ok"], t + 1)
            for h in range(H):
                last = pe.transpose(pb[5 + h // 4][0:QKD, h % 4 * P:(h % 4 + 1) * P], q96[:, h, :], ident)
            last.then_inc(s["qT_ps"], 1)
            f(5)
            wait(pe, s["sig_ok"], t + 1)
            wait(pe, s["kts_ok"], t + 1)
            mm(pb[2][:, :], c_("cum_inc"), sig[:, :])
            mm(pb[7][:, :], c_("cum_exc"), sig[:, :])
            for j in range(4):
                last = mm(pb[3][:, 2 * j:2 * j + 2], sig[:, j * P:(j + 1) * P], c_("chunk"))
            last.then_inc(s["cum_ps"], 1)
            f(6)
            wait(pe, s["pc_ok"], t + 1)
            wait(pe, s["qts_ok"], t + 1)
            for kind, (buf, ok) in enumerate(((aA, "A_ok"), (rR, "R_ok"), (aB, "B_ok"), (kK, "K_ok"))):
                wait(pe, s[ok], t + 1)
                for j in range(4):
                    last = pe.transpose(pb[3 + j][:, kind * P:(kind + 1) * P], buf[:, j * P:(j + 1) * P], ident)
            last.then_inc(s["XT_ps"], 1)
            f(7)
            wait(pe, s["XT_act"], t + 1)
            wait(pe, s["XT_dve"], t + 1)
            apart()
            for h in range(H):
                r, j = slice(64 * (h % 2), 64 * (h % 2) + 64), h // 2
                for c in range(2):
                    q = slice(64 * c, 64 * c + 64)
                    for kind, banks in ((2, (7, 2)), (3, (3, 4))):
                        mm(pb[banks[h % 2]][q, j * P:(j + 1) * P].rearrange("p (a n) -> p a n", a=2),
                           XT[r, j, kind, q], XT[r, j, 0:2, q])
                    last = mm(pb[5 + h % 2][q, j * 64:(j + 1) * 64], XT[r, j, 0, q], XT[r, j, 2, q])
            last.then_inc(s["G_ps"], 1)
            f(8)

            def blocks(bank, left, right):
                for h in range(H):
                    for c in range(2):
                        q = slice(64 * c, 64 * c + 64)
                        last = mm(bank[q, h * 64:(h + 1) * 64], left[q, h, :], right[q, h, :])
                return last

            wait(pe, s["gmask_ok"], t + 1)
            mm(pb[6][:, :], loraT[:, P:2 * P], g2[:, :]).then_inc(s["gate_ps"], 1)
            n_lv = len(LEVELS)
            for i in range(n_lv):
                wait(pe, s["Ls_ok"], t * n_lv + i + 1)
                wait(pe, s["E_ok"], t * (n_lv + 1) + i + 1)
                apart()
                blocks(pb[3], Ls[i % 2], Em).then_inc(s["T1_ps"], 1)
                wait(pe, s["T1_ok"], t * n_lv + i + 1)
                wait(pe, s["D_ok"], t * n_lv + i + 1)
                apart()
                last = blocks(pb[4], Dm, T1h)
                if i < n_lv - 1:
                    last = blocks(pb[5], T1h, Dm)
                last.then_inc(s["ED_ps"], 1)
                if i < 3:
                    f(9 + i)
            wait(pe, s["E_ok"], t * (n_lv + 1) + n_lv + 1)
            V = mixed[b][:, 2 * RW:3 * RW].rearrange("p (h n) -> p h n", h=H)
            for c in range(2):
                q = slice(64 * c, 64 * c + 64)
                S = SS_ if is_first(t) and c == 1 else SP_
                wait(pe, s["S_ok"], t * 2 + c)
                apart()
                if is_first(t) and c == 0:
                    pe.wait_ge(s["init_ok"], 1)
                for j in range(4):
                    pw = slice(j * P, (j + 1) * P)
                    mm(pb[2][q, pw], XT[:, j, 0, q], S[:, j, :], True, False)
                    for h in (2 * j, 2 * j + 1):
                        last = mm(pb[2][q, h * 64:(h + 1) * 64], GK[q, h, 0:64], V[q, h, :], False, h % 2 == 1)
                last.then_inc(s["U_ps"], 1)
                wait(pe, s["U_ok"], t * 2 + c + 1)
                apart()
                for h in range(H):
                    last = mm(pb[3][q, h * 64:(h + 1) * 64], Em[q, h, :], U[q, h * 64:(h + 1) * 64])
                last.then_inc(s["SA_ps"], 1)
                wait(pe, s["SA_ok"], t * 2 + c + 1)
                for j in range(4):
                    pw = slice(j * P, (j + 1) * P)
                    mm(pb[4][:, pw], aB[q, pw], SA[q, pw], True, False)
                    last = mm(pb[4][:, pw], kK[q, pw], mixed[b][q, 2 * RW + j * P:2 * RW + (j + 1) * P], False, True)
                last.then_inc(s["dS_ps"], 1)
                for j in range(4):
                    mm(pb[7][q, j * P:(j + 1) * P], XT[:, j, 1, q], S[:, j, :], True, False)
                    for h in (2 * j, 2 * j + 1):
                        w = slice(h * 64, (h + 1) * 64)
                        mm(pb[7][q, w], GB[q, h, :], SA[q, w], False, False)
                        last = mm(pb[7][q, w], GK[q, h, 64:P], V[q, h, :], False, h % 2 == 1)
                last.then_inc(s["Y_ps"], 1)

        pe.wait_ge(s["s_loaded"], 16 * 8)
        fill(0, 0, 0)
        ssq(0)
        for u in range(1, 2 * IPC):
            fill(0, 0, u)
        tiles(pe, step)
        rw_transposes(TILES - 1)

    @block.scalar
    def _(act):
        run = Chain(act, s["act_chain"], ACT_STEPS)

        def evac(t, b, n):
            if n == 0:
                wait(act, s["rstd_ok"], t + 1)
                if not is_first(t):
                    wait(act, s["sh_in"], t * 32 + 48)
            wait(act, s["ip_ps"], t * IPC + n + 1)
            act.activation(proj[b][:, n * IPW:(n + 1) * IPW], pb[n % 2][:, 0:IPW], ACT.Copy, scale=rstd[b][:, 0:1]
                           ).then_inc(s["p_ok"], 1)

        def rw_evac(t):
            wait(act, s["rwT_ps"], t + 1)
            wait(act, s["st_rw"], t * 16)
            act.activation(rwT[:, :, :], pb[5][:, :].rearrange("p (j n) -> p j n", j=4), ACT.Copy).then_inc(s["rwT_ok"], 1)

        def step(t, b, u):
            run.tile(t)
            pr, xm = proj[b], mixed[b]
            n_lv = len(LEVELS)

            def ev(n):
                if not is_last(t):
                    evac(t + 1, 1 - b, n)

            wait(act, s["p_ok"], t * IPC + IPC)
            run(act.activation(junk[:, 0:QL], pr[:, 0:QL], ACT.Square, accum_out=st3[:, 0:1]))
            run(act.activation(junk[:, 0:KVL], pr[:, QL:QL + KVL], ACT.Square, accum_out=st3[:, 1:2]))
            act.activation(junk[:, 0:ROPE], pr[:, QL + KVL:MLA], ACT.Square, accum_out=st3[:, 2:3]).then_inc(s["lat_ssq"], 1)
            ev(0)
            wait(act, s["latT_ps"], t + 1)
            act.activation(latT[:, :], pb[2][:, 0:QL + KVL], ACT.Copy).then_inc(s["latT_ok"], 1)
            if not is_first(t):
                rw_evac(t - 1)
            wait(act, s["xm_ok"], t + 1)
            run(act.activation(lw[:, 0:LORA], xm[:, 3 * RW:3 * RW + LORA], ACT.Tanh))
            act.activation(lw[:, LORA:P], xm[:, 3 * RW + LORA:3 * RW + P], ACT.Copy).then_inc(s["lw_ok"], 1)
            act.activation(sg[:, :], xm[:, 3 * RW + P:], ACT.Tanh, scale=0.5).then_inc(s["sg_e"], 1)
            wait(act, s["up_ps"], t + 1)
            kv = [pb[3 + i][:, :].rearrange("p (h n) -> p h n", h=4) for i in range(2)]
            qp = [pb[5 + i][:, 0:384].rearrange("p (h n) -> p h n", h=4) for i in range(2)]
            run(act.activation(sqk[:, 0:4, :], kv[0][:, :, 0:NOPE], ACT.Square))
            act.activation(sqk[:, 4:8, :], kv[1][:, :, 0:NOPE], ACT.Square).then_inc(s["sqk_ok"], 1)
            run(act.activation(sqq[:, 0:4, :], qp[0], ACT.Square))
            act.activation(sqq[:, 4:8, :], qp[1], ACT.Square).then_inc(s["sqq_ok"], 1)
            run(act.activation(vst[:, 0:4, :], kv[0][:, :, NOPE:], ACT.Copy))
            act.activation(vst[:, 4:8, :], kv[1][:, :, NOPE:], ACT.Copy).then_inc(s["v_ok"], 1)
            ev(1)
            wait(act, s["loraT_ps"], t + 1)
            act.activation(loraT[:, :], pb[7][:, 0:2 * P], ACT.Copy).then_inc(s["loraT_ok"], 1)
            wait(act, s["z_ok"], t + 1)
            act.activation(sig[:, :], sig[:, :], ACT.Tanh, scale=0.5).then_inc(s["z_e"], 1)
            wait(act, s["a_ok_z"], t + 1)
            act.activation(aB[:, :], aB[:, :], ACT.Tanh, scale=0.5).then_inc(s["a_e"], 1)
            wait(act, s["kkr_ok"], t + 1)
            act.activation(tmp[:, :], kk[:, :], ACT.Square).then_inc(s["kksq_ok"], 1)
            wait(act, s["kT_ps"], t + 1)
            run(act.activation(kts[:, 0:4, :], pb[3][0:QKD, :].rearrange("p (h n) -> p h n", h=4), ACT.Copy))
            act.activation(kts[:, 4:8, :], pb[4][0:QKD, :].rearrange("p (h n) -> p h n", h=4), ACT.Copy).then_inc(s["kts_ok"], 1)
            wait(act, s["qT_ps"], t + 1)
            run(act.activation(qts[:, 0:4, :], pb[5][0:QKD, :].rearrange("p (h n) -> p h n", h=4), ACT.Copy))
            last = act.activation(qts[:, 4:8, :], pb[6][0:QKD, :].rearrange("p (h n) -> p h n", h=4), ACT.Copy)
            if is_first(t):
                last.then_inc(s["act_once"], 1)
                act.wait_ge(s["act_once"], 1)
                act.activation(g.k_new[:, :, :], kts[:, :, SAMPLE_ROW:SAMPLE_ROW + SAMPLE], ACT.Copy).then_inc(s["act_once"], 1)
                last = act.activation(g.q_new[:, :, :], qts[:, :, SAMPLE_ROW:SAMPLE_ROW + SAMPLE], ACT.Copy)
            last.then_inc(s["qts_ok"], 1)
            ev(2)
            wait(act, s["cum_ps"], t + 1)
            act.activation(rR[:, :], pb[2][:, :], ACT.Exp).then_inc(s["rR_e"], 1)
            act.activation(kK[:, :], pb[2][:, :], ACT.Exp, scale=-1.0).then_inc(s["kK_e"], 1)
            act.activation(aA[:, :], pb[7][:, :], ACT.Exp).then_inc(s["aA_e"], 1)
            act.activation(pc[:, :], pb[3][:, 0:8], ACT.Exp).then_inc(s["pc_ok"], 1)
            wait(act, s["XT_ps"], t + 1)
            run(act.activation(XT[:, 0], pb[3][:, :].rearrange("p (a n) -> p a n", a=4), ACT.Copy))
            act.activation(XT[:, 1], pb[4][:, :].rearrange("p (a n) -> p a n", a=4), ACT.Copy).then_inc(s["XT_act"], 1)
            ev(3)
            wait(act, s["G_ps"], t + 1)
            wait(act, s["st_kv"], t * 48 + 48)
            run(act.activation(Lraw[:, 0::2, :], pb[5][:, 0:256].rearrange("p (h n) -> p h n", h=4), ACT.Copy))
            act.activation(Lraw[:, 1::2, :], pb[6][:, 0:256].rearrange("p (h n) -> p h n", h=4), ACT.Copy).then_inc(s["Lraw_ok"], 1)
            for i in range(n_lv):
                wait(act, s["ED_ps"], t * n_lv + i + 1)
                act.activation(Em, pb[4][:, :].rearrange("p (h n) -> p h n", h=H), ACT.Copy).then_inc(s["E_ok"], 1)
                if i == 0:
                    ev(4)
                if i == 2:
                    ev(5)
            for c in range(2):
                wait(act, s["U_ps"], t * 2 + c + 1)
                q = slice(64 * c, 64 * c + 64)
                act.activation(U[q, :], pb[2][q, :], ACT.Copy).then_inc(s["U_ok"], 1)
            wait(act, s["yc_ok"], t + 1)
            act.activation(tmp[:, :], yb[:, :], ACT.Square).then_inc(s["ysq_ok"], 1)

        for n in range(IPC):
            evac(0, 0, n)
        tiles(act, step)
        run.tile(0)
        rw_evac(TILES - 1)

    @block.gpsimd
    def _(pool):
        run = Chain(pool, s["pool_chain"], POOL_STEPS)
        tt = pool.tensor_tensor

        def rsqrt(out, ms, ok, ready, t, n):
            wait(pool, s[ready], t + 1)
            tt(out, ms, c_("minus_half")[:, 0:n], ALU.pow).then_inc(s[ok], 1)

        def scale_x(t, b, u):
            wait(pool, s[f"x_in{b}"], u * 16 + 16)
            wait(pool, s["ssq_ps"], t)
            tt(xsq[:, :, :], xt[b][:, :, :], xt[b][:, :, :], ALU.mult).then_inc(s["x_squared"], 1)
            pool.wait_ge(s["x_squared"], t + 1)
            tt(xt[b][:, :, :], xt[b][:, :, :], bcast(gmix[:, :], 2, P), ALU.mult).then_inc(s["x_scaled"], 1)

        def step(t, b, u):
            run.tile(t)
            pr, xm = proj[b][:, MLA:], mixed[b]
            r, k, v = (xm[:, i * RW:(i + 1) * RW] for i in range(3))
            if not is_last(t):
                rsqrt(rstd[1 - b][:, :], mean_sq[:, :], "rstd_ok", "mean_ok", t + 1, 1)
            rsqrt(st3[:, :], st3[:, :], "st3_ok", "st3_ms", t, 3)
            wait(pool, s["sh_in"], t * 32 + 80)
            run(tt(xm[:, :], xm[:, :], pr, ALU.subtract))
            run(tt(xm[:, :], xm[:, :], v_("mu_shift"), ALU.mult))
            tt(xm[:, :], xm[:, :], pr, ALU.add).then_inc(s["xm_ok"], 1)
            pool.wait_ge(s["xm_ok"], t + 1)
            wait(pool, s["rw_ok"], t)
            tt(kk[:, :], k, v_("k_k"), ALU.mult).then_inc(s["kkr_ok"], 1)
            rsqrt(st24[:, :], st24[:, :], "st24_ok", "st24_ms", t, 24)
            if not is_last(t, 2):
                scale_x(t + 2, b, u + 1)
            rsqrt(n8[:, :], n8[:, :], "n8_ok", "n8_ms", t, 8)
            wait(pool, s["kk_ok"], t + 1)
            wait(pool, s["a_ok"], t + 1)
            wait(pool, s["keff_ok"], t + 1)
            tt(aB[:, :], aB[:, :], kk[:, :], ALU.mult).then_inc(s["kka_ok"], 1)
            run(tt(tmp[:, :], r, v_("r_k"), ALU.mult))
            tt(tmp[:, :], tmp[:, :], keff[:, :], ALU.mult).then_inc(s["rk_ok"], 1)
            wait(pool, s["rR_e"], t + 1)
            tt(rR[:, :], rR[:, :], r, ALU.mult).then_inc(s["R_ok"], 1)
            wait(pool, s["bon_ok"], t + 1)
            wait(pool, s["A_ok"], t + 1)
            tt(heads(kk[:, :]), heads(v), bcast(b8[:, :], 2, CHUNK), ALU.mult).then_inc(s["bonv_ok"], 1)
            wait(pool, s["Lraw_ok"], t + 1)
            n_lv = len(LEVELS)
            for i in range(n_lv):
                if i >= 2:
                    wait(pool, s["T1_ps"], t * n_lv + i - 1)
                tt(Ls[i % 2], Lraw, bcast(c_("levels")[:, i * 64:(i + 1) * 64], 1, H), ALU.mult).then_inc(s["Ls_ok"], 1)
            rsqrt(v8[:, :], v8[:, :], "v8_ok", "v8_ms", t, 8)

        pool.memset(SP_[:, :, :], 0.0).then_inc(s["pool_once"], 1)
        pool.memset(mixed[0][0:1, :], 0.0).then_inc(s["pool_once"], 1)
        pool.wait_ge(s["pool_once"], 2)
        pool.sem_inc(s["init_ok"], 1)
        pool.wait_ge(s["s_loaded"], 16 * 8)
        scale_x(0, 0, 0)
        rsqrt(rstd[0][:, :], mean_sq[:, :], "rstd_ok", "mean_ok", 0, 1)
        scale_x(1, 1, 0)
        tiles(pool, step)
        run.tile(0)

    @block.vector
    def _(dve):
        run = Chain(dve, s["dve_chain"], DVE_STEPS)
        tt, ts, stt = dve.tensor_tensor, dve.tensor_scalar, dve.scalar_tensor_tensor
        red = lambda out, in_: dve.tensor_reduce(out, in_, AX.X, ALU.add)

        def named(ins, name, value):
            ins.then_inc(s[name], 1)
            dve.wait_ge(s[name], value)

        def row_rms(t, b):
            wait(dve, s["ssq_ps"], t + 1)
            ts(mean_sq[:, :], pb[1][:, 400:401], 1.0 / D, EPS, ALU.mult, ALU.add).then_inc(s["mean_ok"], 1)

        def step(t, b, u):
            run.tile(t)
            pr, xm = proj[b], mixed[b]
            r, k, v = (xm[:, i * RW:(i + 1) * RW] for i in range(3))
            n_lv = len(LEVELS)
            if not is_last(t):
                row_rms(t + 1, 1 - b)
            wait(dve, s["lat_ssq"], t + 1)
            if not is_first(t):
                wait(dve, s["st_lat"], t * 32 + 32)
            run(tt(st3[:, :], st3[:, :], c_("inv3"), ALU.mult))
            ts(st3[:, :], st3[:, :], EPS, None, ALU.add).then_inc(s["st3_ms"], 1)
            wait(dve, s["st3_ok"], t + 1)
            run(stt(lat[:, 0:QL], pr[:, 0:QL], st3[:, 0:1], v_("q_norm_g"), ALU.mult, ALU.mult))
            named(stt(lat[:, QL:], pr[:, QL:QL + KVL], st3[:, 1:2], v_("kv_norm_g"), ALU.mult, ALU.mult), "lat_ok", t + 1)
            run(stt(krn[:, 0, :], pr[:, QL + KVL:MLA], st3[:, 2:3], v_("kn_rope_g"), ALU.mult, ALU.mult))
            tb = tab(t)
            run(tt(krn[:, 1, :], krn[:, 0, :], tb[:, 0:ROPE], ALU.mult))
            run(tt(krn[:, 2, :], krn[:, 0, :], tb[:, ROPE:], ALU.mult))
            run(tt(kr[:, 0:half], krn[:, 1, 0:half], krn[:, 2, half:], ALU.add))
            named(tt(kr[:, half:], krn[:, 1, half:], krn[:, 2, 0:half], ALU.add), "kr_ok", t + 1)
            wait(dve, s["sg_e"], t + 1)
            named(ts(sg[:, :], sg[:, :], 0.5, 0.5, ALU.mult, ALU.add), "sg_ok", t + 1)
            kv = [pb[3 + i][:, :].rearrange("p (h n) -> p h n", h=4) for i in range(2)]
            qp = [pb[5 + i][:, 0:384].rearrange("p (h n) -> p h n", h=4) for i in range(2)]
            wait(dve, s["sqk_ok"], t + 1)
            run(red(st24[:, 0:8], sqk))
            wait(dve, s["sqq_ok"], t + 1)
            run(red(st24[:, 8:16], sqq[:, :, 0:NOPE]))
            run(red(st24[:, 16:24], sqq[:, :, NOPE:]))
            run(tt(st24[:, :], st24[:, :], c_("inv24"), ALU.mult))
            ts(st24[:, :], st24[:, :], EPS, None, ALU.add).then_inc(s["st24_ms"], 1)
            wait(dve, s["st24_ok"], t + 1)
            wait(dve, s["v_ok"], t + 1)
            for i in range(2):
                run(tt(k96[:, 4 * i:4 * i + 4, 0:NOPE], kv[i][:, :, 0:NOPE], bcast(st24[:, 4 * i:4 * i + 4], 2, NOPE), ALU.mult))
            named(dve.tensor_copy(k96[:, :, NOPE:], bcast(kr[:, :], 1, H)), "k96_ok", t + 1)
            wait(dve, s["lora_ps"], t + 1)
            named(tt(sig[:, :], pb[2][:, :], v_("w0"), ALU.add), "z_ok", t + 1)
            named(tt(aB[:, :], pb[7][:, :], v_("a0"), ALU.add), "a_ok_z", t + 1)
            for i in range(2):
                run(tt(q96[:, 4 * i:4 * i + 4, 0:NOPE], qp[i][:, :, 0:NOPE], bcast(st24[:, 8 + 4 * i:12 + 4 * i], 2, NOPE), ALU.mult))
                run(tt(q96[:, 4 * i:4 * i + 4, NOPE:], qp[i][:, :, NOPE:], bcast(st24[:, 16 + 4 * i:20 + 4 * i], 2, ROPE), ALU.mult))
            run(tt(q96[:, :, 0:NOPE], q96[:, :, 0:NOPE], bcast(g_qk[:, :], 1, H), ALU.mult))
            run(tt(q96[:, :, NOPE:], q96[:, :, NOPE:], bcast(v_("qn_rope_g"), 1, H), ALU.mult))
            rot = q96[:, :, NOPE:]
            run(tt(rope2[:, 0], rot, bcast(tb[:, 0:ROPE], 1, H), ALU.mult))
            run(tt(rope2[:, 1], rot, bcast(tb[:, ROPE:], 1, H), ALU.mult))
            run(tt(rot[:, :, 0:half], rope2[:, 0, :, 0:half], rope2[:, 1, :, half:], ALU.add))
            named(tt(rot[:, :, half:], rope2[:, 0, :, half:], rope2[:, 1, :, 0:half], ALU.add), "q96_ok", t + 1)
            wait(dve, s["z_e"], t + 1)
            last = ts(sig[:, :], sig[:, :], 0.5, 0.5, ALU.mult, ALU.add)
            if is_first(t):
                last.then_inc(s["dve_once"], 1)
                dve.wait_ge(s["dve_once"], 2)
                last = ts(sig[:, :], sig[:, :], c_("live"), None, ALU.mult)
            named(last, "sig_ok", t + 1)
            wait(dve, s["a_e"], t + 1)
            named(ts(aB[:, :], aB[:, :], 0.5, 0.5, ALU.mult, ALU.add), "a_ok", t + 1)
            wait(dve, s["kksq_ok"], t + 1)
            run(red(n8[:, :], heads(tmp[:, :])))
            ts(n8[:, :], n8[:, :], 1e-24, None, ALU.max).then_inc(s["n8_ms"], 1)
            wait(dve, s["n8_ok"], t + 1)
            named(tt(heads(kk[:, :]), heads(kk[:, :]), bcast(n8[:, :], 2, CHUNK), ALU.mult), "kk_ok", t + 1)
            run(stt(keff[:, :], aB[:, :], -1.0, v_("k_a"), ALU.add, ALU.mult))
            named(stt(keff[:, :], keff[:, :], 1.0, k, ALU.add, ALU.mult), "keff_ok", t + 1)
            wait(dve, s["aA_e"], t + 1)
            wait(dve, s["kka_ok"], t + 1)
            named(stt(aA[:, :], kk[:, :], -1.0, aA[:, :], ALU.mult, ALU.mult), "A_ok", t + 1)
            wait(dve, s["kK_e"], t + 1)
            if is_first(t):
                ts(kK[:, :], kK[:, :], c_("live"), None, ALU.mult).then_inc(s["dve_once"], 1)
                dve.wait_ge(s["dve_once"], 3)
            named(tt(aB[:, :], aB[:, :], kK[:, :], ALU.mult), "B_ok", t + 1)
            named(tt(kK[:, :], keff[:, :], kK[:, :], ALU.mult), "K_ok", t + 1)
            wait(dve, s["rk_ok"], t + 1)
            named(red(b8[:, :], heads(tmp[:, :])), "bon_ok", t + 1)
            wait(dve, s["XT_ps"], t + 1)
            wait(dve, s["st_kv"], t * 48 + 48)
            run(dve.tensor_copy(XT[:, 2], pb[5][:, :].rearrange("p (a n) -> p a n", a=4)))
            named(dve.tensor_copy(XT[:, 3], pb[6][:, :].rearrange("p (a n) -> p a n", a=4)), "XT_dve", t + 1)
            wait(dve, s["G_ps"], t + 1)
            for i, bank in enumerate((7, 2)):
                g4 = pb[bank][:, :].rearrange("p (h n) -> p h n", h=4)
                run(tt(Em[:, i::2, :], g4[:, :, 0:64], bcast(c_("b_mask")[:, 0:64], 1, 4), ALU.mult))
                run(tt(GB[:, i::2, :], g4[:, :, 64:], bcast(c_("b_mask")[:, 64:], 1, 4), ALU.mult))
            named(tt(Em, Em, bcast(c_("eye"), 1, H), ALU.add), "E_ok", t * (n_lv + 1) + 1)
            run(tt(GK[:, 0::2, :], pb[3][:, :].rearrange("p (h n) -> p h n", h=4), bcast(c_("k_mask"), 1, 4), ALU.mult))
            run(tt(GK[:, 1::2, :], pb[4][:, :].rearrange("p (h n) -> p h n", h=4), bcast(c_("k_mask"), 1, 4), ALU.mult))
            wait(dve, s["Lraw_ok"], t + 1)
            run(tt(Dm, Lraw, bcast(c_("first"), 1, H), ALU.mult))
            named(tt(Dm, Dm, bcast(c_("eye"), 1, H), ALU.add), "D_ok", t * n_lv + 1)
            wait(dve, s["pc_ok"], t + 1)
            named(tt(pcm[:, :, :, :], bcast(pc[:, :].rearrange("p (j c) -> p c j", c=2), 3, 2),
                     bcast(bcast(c_("own"), 1, 4), 1, 2), ALU.mult), "gmask_ok", t + 1)
            for i in range(n_lv):
                wait(dve, s["T1_ps"], t * n_lv + i + 1)
                named(tt(T1h, pb[3][:, :].rearrange("p (h n) -> p h n", h=H), bcast(c_("eye"), 1, H), ALU.add), "T1_ok", t * n_lv + i + 1)
                wait(dve, s["ED_ps"], t * n_lv + i + 1)
                if i < n_lv - 1:
                    named(dve.tensor_copy(Dm, pb[5][:, :].rearrange("p (h n) -> p h n", h=H)), "D_ok", t * n_lv + i + 2)
            for c in range(2):
                q = slice(64 * c, 64 * c + 64)
                S = SS_ if is_first(t) and c == 1 else SP_
                wait(dve, s["SA_ps"], t * 2 + c + 1)
                named(dve.tensor_copy(SA[q, :], pb[3][q, :]), "SA_ok", t * 2 + c + 1)
                wait(dve, s["dS_ps"], t * 2 + c + 1)
                wait(dve, s["Y_ps"], t * 2 + c + 1)
                run(tt(S[:, :, :], S[:, :, :], pb[4][:, :].rearrange("p (j n) -> p j n", j=4), ALU.add))
                s8 = S[:, :, :].rearrange("p j (a n) -> p (j a) n", a=2)
                named(tt(s8, s8, bcast(pcm[:, c].rearrange("p j a -> p (j a)"), 2, CHUNK), ALU.mult), "S_ok", t * 2 + c + 1)
            y = pb[7][:, :].rearrange("p (h n) -> p h n", h=H)
            ybh = heads(yb[:, :])
            if not is_first(t):
                wait(dve, s["rwT_ps"], t)
            run(red(y8[:, :], y))
            run(ts(y8[:, :], y8[:, :], -1.0 / CHUNK, None, ALU.mult))
            named(tt(ybh, y, bcast(y8[:, :], 2, CHUNK), ALU.add), "yc_ok", t + 1)
            wait(dve, s["ysq_ok"], t + 1)
            run(red(v8[:, :], heads(tmp[:, :])))
            ts(v8[:, :], v8[:, :], 1.0 / CHUNK, LNX_EPS, ALU.mult, ALU.add).then_inc(s["v8_ms"], 1)
            wait(dve, s["v8_ok"], t + 1)
            run(tt(ybh, ybh, bcast(v8[:, :], 2, CHUNK), ALU.mult))
            run(tt(yb[:, :], yb[:, :], v_("lnx_g"), ALU.mult))
            run(tt(yb[:, :], yb[:, :], v_("lnx_b"), ALU.add))
            wait(dve, s["bonv_ok"], t + 1)
            run(tt(yb[:, :], yb[:, :], kk[:, :], ALU.add))
            wait(dve, s["gate_ps"], t + 1)
            named(tt(yb[:, :], yb[:, :], pb[6][:, :], ALU.mult), "rw_ok", t + 1)

        dve.wait_ge(s["s_loaded"], 16 * 8)
        tt(g_qk[:, :], v_("qn_nope_g"), v_("kn_nope_g"), ALU.mult).then_inc(s["dve_once"], 1)
        dve.wait_ge(s["dve_once"], 1)
        row_rms(0, 0)
        tiles(dve, step)
        run.tile(0)


def credit(e, sem, n):
    for _ in range(n):
        e.nop().then_inc(sem, 1)


def prompt_attention(nc, g, io, phase):
    sb, sem, pb, con = phase.sb, g.sem, g.pb, g.con
    QT_N = SEQ // P
    qT = [sb(f"qT{i}", [P, SEQ]) for i in range(2)]
    kT = [sb(f"kT{i}", [P, KEYS]) for i in range(2)]
    vh = [sb(f"vh{i}", [P, TILES, VD + 1]) for i in range(2)]
    at = [sum(SEQ - P * j for j in range(kt)) for kt in range(QT_N + 1)]
    pT = sb("pT", [P, at[-1]])
    pM = sb("pM", [META, SEQ])
    attn = sb("attn", [P, QT_N, MLA_OUT])
    part = sb("part", [P, QT_N, 4])
    neg_max = sb("neg_max", [P, QT_N])
    inv = sb("inv", [P, QT_N])
    norm = sb("norm", [P, QT_N])
    junk = sb("junk2", [P, MLA_OUT])
    g_attn = sb("g_attn", [P, 4])
    ident = con[:, CON["ident"][0]:CON["ident"][0] + P]
    minus_half = con[:, CON["minus_half"][0]:CON["minus_half"][0] + QT_N]
    units_b = [(kt, a, min(512, SEQ - a)) for kt in [None, *range(QT_N)] for a in range((kt or 0) * P, SEQ, 512)]
    units_a = []
    for t in range(QT_N):
        w = META + (t + 1) * P
        n = -(-w // 512)
        cuts = [w * j // n for j in range(n + 1)]
        units_a += [(t, j, cuts[j], cuts[j + 1], j == n - 1) for j in range(n)]
    NB, NA, NR = len(units_b), len(units_a), 2
    RING = 6
    bank_b = [pb[u % RING] for u in range(NB)]
    bank_a = [pb[(NB + u) % RING] for u in range(NA)]
    bank_r = [pb[(NB + NA + u) % RING] for u in range(NR)]
    assert (NB + NA + NR) % RING == 0
    parts_out = [(QT_N // 2, QT_N, 7), (0, QT_N // 2, 6)]
    s = {n: sem("a_" + n) for n in """qk_in0 qk_in1 v_in0 v_in1 rw_in waited fixed b_ps b_ok a_ps a_ok max_ok neg_ok r_ps r_ok
        pv_ps inv_ok o_ok sq_ok ms2 ms_ok scaled mt_ps mt_ok part_ok""".split()}
    block = phase.block()

    def before(pos, head):
        pos, head = (pos - RING, head) if pos >= RING else (pos - RING + NB + NA + NR, head - 1)
        if pos < NB:
            return s["b_ok"], head * NB + pos + 1
        if pos < NB + NA:
            return s["a_ok"], (head + 1) * NA + (pos - NB) + 1
        return s["r_ok"], (head + 1) * NR + (pos - NB - NA) + 1

    @block.sync
    def _(sp):
        def load_qk(i, b):
            head = i * 2 + b
            sp.dma_start(qT[b][0:QKD, :], io.qT[:, bass.ds(head, 1), :].rearrange("d h n -> d (h n)")).then_inc(s[f"qk_in{b}"], 16)
            sp.dma_start(kT[b][0:QKD, :], io.kT[:, bass.ds(head, 1), :].rearrange("d h n -> d (h n)")).then_inc(s[f"qk_in{b}"], 16)

        def load_v(i, b):
            head = i * 2 + b
            sp.dma_start(vh[b][:, 1:, 0:VD], io.v[1:, :, bass.ds(head, 1), :].rearrange("t p h d -> p t (h d)")).then_inc(s[f"v_in{b}"], 16)
            sp.dma_start(vh[b][0:META, 0, 0:VD], io.v[0, 0:META, bass.ds(head, 1), :].rearrange("p h d -> p (h d)")).then_inc(s[f"v_in{b}"], 16)

        for b in range(2):
            load_qk(0, b)
        for b in range(2):
            load_v(0, b)
        sp.dma_start(g_attn[:, :], io.g_attn).then_inc(s["rw_in"], 16)
        sp.dma_start(g.mixT[:, 4:, 0:SEQ], io.rwT[:, :, P:]).then_inc(s["rw_in"], 16)
        sp.dma_start(g.mixT[:, 4:, SEQ:], io.rwT[:, :, SAMPLE_ROW:SAMPLE_ROW + SAMPLE]).then_inc(s["rw_in"], 16)
        with sp.Fori(0, H // 2 - 1) as i:
            for b in range(2):
                sp.wait_ge(s["b_ps"], (i * 2 + b + 1) * NB)
                sp.nop().then_inc(s["waited"], 1)
                load_qk(i + 1, b)
                sp.wait_ge(s["pv_ps"], (i * 2 + b) * 2 + 2)
                sp.nop().then_inc(s["waited"], 1)
                load_v(i + 1, b)
        sp.wait_ge(s["rw_in"], 48)

    @block.tensor
    def _(pe):
        def unit_a(b, u):
            t, _, x, y, _ = units_a[u]
            pe.matmul(bank_a[u][:, 0:y - x], qT[b][0:QKD, t * P:(t + 1) * P], kT[b][0:QKD, x:y], start=True, stop=True
                      ).then_inc(s["a_ps"], 1)

        def rows(head, b):
            pe.wait_ge(s["neg_ok"], head + 1)
            for u in range(NR):
                pe.wait_ge(*before(NB + NA + u, head - 1))
                for x in range(4):
                    last = pe.transpose(bank_r[u][0:1, x * P:(x + 1) * P], neg_max[:, 4 * u + x:4 * u + x + 1], ident)
                last.then_inc(s["r_ps"], 1)

        def head_steps(i, b, more):
            head = i * 2 + b
            pe.wait_ge(s["r_ok"], head * NR + NR)
            for u, (kt, a, n) in enumerate(units_b):
                pe.wait_ge(*before(u, head))
                m = META if kt is None else P
                k = kT[b][:, 0:META] if kt is None else kT[b][:, META + kt * P:META + (kt + 1) * P]
                pe.matmul(bank_b[u][0:m, 0:n], k, qT[b][:, a:a + n], start=True, stop=True).then_inc(s["b_ps"], 1)
            if more:
                pe.wait_ge(s[f"qk_in{1 - b}"], (i + b) * 32 + 32)
                for u in range(NA):
                    pe.wait_ge(*before(NB + u, head))
                    unit_a(1 - b, u)
            pe.wait_ge(s["b_ok"], head * NB + NB)
            pe.wait_ge(s[f"v_in{b}"], i * 32 + 32)
            for j, (t0, t1, bank) in enumerate(parts_out):
                pe.wait_ge(s["o_ok"], head * 2 + j + 1)
                for t in range(t0, t1):
                    out = pb[bank][:, (t - t0) * (VD + 1):(t - t0 + 1) * (VD + 1)]
                    for kt in range(t + 1):
                        x = at[kt] + (t - kt) * P
                        pe.matmul(out, pT[:, x:x + P], vh[b][:, 1 + kt, :], start=kt == 0, stop=False)
                    last = pe.matmul(out, pM[:, t * P:(t + 1) * P], vh[b][0:META, 0, :], start=False, stop=True)
                last.then_inc(s["pv_ps"], 1)
                if more and j == 0:
                    rows(head + 1, 1 - b)

        pe.wait_ge(s["fixed"], 6)
        pe.wait_ge(s["qk_in0"], 32)
        for u in range(NA):
            if u >= RING:
                pe.wait_ge(s["a_ok"], u - RING + 1)
            unit_a(0, u)
        rows(0, 0)
        with pe.Fori(0, H // 2 - 1) as i:
            for b in range(2):
                head_steps(i, b, True)
        head_steps(H // 2 - 1, 0, True)
        head_steps(H // 2 - 1, 1, False)
        for t in range(QT_N):
            pe.wait_ge(s["scaled"], t + 1)
            if t >= 2:
                pe.wait_ge(s["mt_ok"], t - 1)
            for j in range(4):
                last = pe.transpose(pb[6 + t % 2][:, j * P:(j + 1) * P], attn[:, t, j * P:(j + 1) * P], ident)
            last.then_inc(s["mt_ps"], 1)

    @block.scalar
    def _(act):
        def rows(head, b):
            for u in range(NR):
                act.wait_ge(s["r_ps"], head * NR + u + 1)
                act.activation(qT[b][QKD:QKD + 1, u * 512:(u + 1) * 512], bank_r[u][0:1, :], ACT.Copy).then_inc(s["r_ok"], 1)

        def head_steps(i, b, more):
            head = i * 2 + b
            for u, (kt, a, n) in enumerate(units_b):
                act.wait_ge(s["b_ps"], head * NB + u + 1)
                if kt is None:
                    act.activation(pM[:, a:a + n], bank_b[u][0:META, 0:n], ACT.Exp, scale=ATTN_SCALE).then_inc(s["b_ok"], 1)
                    continue
                x, skip = at[kt] + a - kt * P, 0
                if a == kt * P:
                    skip = CHUNK
                    act.activation(pT[0:CHUNK, x:x + skip], bank_b[u][0:CHUNK, 0:skip], ACT.Exp, scale=ATTN_SCALE)
                act.activation(pT[:, x + skip:x + n], bank_b[u][:, skip:n], ACT.Exp, scale=ATTN_SCALE).then_inc(s["b_ok"], 1)
            if more:
                rows(head + 1, 1 - b)

        act.wait_ge(s["fixed"], 6)
        rows(0, 0)
        with act.Fori(0, H // 2 - 1) as i:
            for b in range(2):
                head_steps(i, b, True)
        head_steps(H // 2 - 1, 0, True)
        head_steps(H // 2 - 1, 1, False)
        for t in range(QT_N):
            act.wait_ge(s["o_ok"], 2 * H + 2)
            act.activation(junk[:, :], attn[:, t, :], ACT.Square, accum_out=norm[:, t:t + 1]).then_inc(s["sq_ok"], 1)
            act.wait_ge(s["sq_ok"], t + 1)

    @block.gpsimd
    def _(pool):
        pool.wait_ge(s["ms2"], 1)
        pool.tensor_tensor(norm[:, :], norm[:, :], minus_half, ALU.pow).then_inc(s["ms_ok"], 1)

    @block.vector
    def _(dve):
        def maxima(head):
            for u, (t, slot, x, y, end) in enumerate(units_a):
                dve.wait_ge(s["a_ps"], head * NA + u + 1)
                w = y - x - (CHUNK if end else 0)
                last = dve.tensor_reduce(part[:, t, slot:slot + 1], bank_a[u][:, 0:w], AX.X, ALU.max)
                if end:
                    last = dve.tensor_reduce(part[CHUNK:P, t, 3:4], bank_a[u][CHUNK:P, w:y - x], AX.X, ALU.max)
                last.then_inc(s["a_ok"], 1)
            dve.wait_ge(s["a_ok"], head * NA + NA)
            dve.tensor_reduce(neg_max[:, :], part[:, :, :], AX.X, ALU.max).then_inc(s["max_ok"], 1)
            dve.wait_ge(s["max_ok"], head + 1)
            dve.tensor_scalar(neg_max[:, :], neg_max[:, :], -1.0, None, ALU.mult).then_inc(s["neg_ok"], 1)

        def head_steps(i, b, more):
            head = i * 2 + b
            if more:
                maxima(head + 1)
            for j, (t0, t1, bank) in enumerate(parts_out):
                out = pb[bank][:, 0:(t1 - t0) * (VD + 1)].rearrange("p (t d) -> p t d", d=VD + 1)
                dve.wait_ge(s["pv_ps"], head * 2 + j + 1)
                dve.reciprocal(inv[:, t0:t1], out[:, :, VD:].rearrange("p t d -> p (t d)")).then_inc(s["inv_ok"], 1)
                dve.wait_ge(s["inv_ok"], head * 2 + j + 1)
                dve.tensor_tensor(attn[:, t0:t1, bass.ds(head * VD, VD)], out[:, :, 0:VD], bcast(inv[:, t0:t1], 2, VD), ALU.mult
                                  ).then_inc(s["o_ok"], 1)

        for b in range(2):
            dve.memset(qT[b][QKD:P, :], 0.0).then_inc(s["fixed"], 1)
            dve.memset(kT[b][QKD:P, :], 0.0).then_inc(s["fixed"], 1)
        dve.wait_ge(s["fixed"], 4)
        for b in range(2):
            dve.memset(kT[b][QKD:QKD + 1, :], 1.0)
            dve.memset(vh[b][:, :, VD:], 1.0)
        for kt in range(QT_N):
            last = dve.memset(pT[CHUNK:P, at[kt]:at[kt] + CHUNK], 0.0)
        last.then_inc(s["fixed"], 2)
        credit(dve, s["o_ok"], 2)
        dve.memset(part[:, :, :], -3.0e38).then_inc(s["part_ok"], 1)
        dve.wait_ge(s["part_ok"], 1)
        maxima(0)
        with dve.Fori(0, H // 2 - 1) as i:
            for b in range(2):
                head_steps(i, b, True)
        head_steps(H // 2 - 1, 0, True)
        head_steps(H // 2 - 1, 1, False)
        dve.wait_ge(s["sq_ok"], QT_N)
        dve.tensor_scalar(norm[:, :], norm[:, :], 1.0 / MLA_OUT, EPS, ALU.mult, ALU.add).then_inc(s["ms2"], 1)
        dve.wait_ge(s["ms_ok"], 1)
        dve.wait_ge(s["rw_in"], 48)
        for t in range(QT_N + 1):
            if t < QT_N:
                dve.tensor_scalar(attn[:, t, :], attn[:, t, :], norm[:, t:t + 1], None, ALU.mult).then_inc(s["scaled"], 1)
            if t:
                dve.wait_ge(s["mt_ps"], t)
                dve.tensor_tensor(g.mixT[:, 0:4, (t - 1) * P:t * P], pb[6 + (t - 1) % 2][:, :].rearrange("p (j n) -> p j n", j=4),
                                  bcast(g_attn[:, :], 2, P), ALU.mult).then_inc(s["mt_ok"], 1)


def sample_attention(nc, g, io, phase):
    sb, sem, pb, con = phase.sb, g.sem, g.pb, g.con
    CT = PAST // P
    ALL = PAST + SAMPLE
    cT = [sb(f"cT{i}", [P, P]) for i in range(2)]
    krc = [sb(f"krc{i}", [P, ROPE]) for i in range(2)]
    sq = sb("sq", [P, H, NOPE])
    r8 = sb("r8", [P, 8])
    k96 = sb("k96c", [P, H, QKD])
    kTc = [sb(f"kTc{i}", [QKD, H, P]) for i in range(2)]
    vc = sb("vc", [P, CT, H * VD])
    sc = sb("sc", [P, 2, ALL])
    pTc = sb("pTc", [P, CT + 1, P])
    top = sb("topc", [P, 2])
    total = sb("totalc", [P, 2])
    osn = sb("osn", [P, 2, VD])
    at_s = sb("at_s", [SAMPLE, H * VD])
    junk = sb("junkc", [SAMPLE, H * VD])
    norm = sb("normc", [SAMPLE, 1])
    g_attn = sb("g_attnc", [P, 4])
    ident = con[:, CON["ident"][0]:CON["ident"][0] + P]
    minus_half = con[:, CON["minus_half"][0]:CON["minus_half"][0] + 8]
    s = {n: sem("c_" + n) for n in """in0 in1 g_in kv_ps sq_ok v_ok red_ok ms_ok r_ok k_a k_b k96_ok kT_ps kT_a kT_b sc_ps sc_ok
        waited new_ps new_ok top1 top_ok p_ok tr_ps ev0 ev1 o_ps l_ok osn_ok at_in asq_ok am_ok ar_ok as_ok at_ps at_ok""".split()}
    block = phase.block()

    def cache_tiles(e, step):
        step(0, 0, 0)
        step(1, 1, 0)
        with e.Fori(1, CT // 2 - 1) as i:
            step(i * 2, 0, i)
            step(i * 2 + 1, 1, i)
        step(CT - 2, 0, CT // 2 - 1)
        step(CT - 1, 1, CT // 2 - 1)

    @block.sync
    def _(sp):
        sp.dma_start(g_attn[:, :], io.g_attn).then_inc(s["g_in"], 16)

        def step(u, b, i):
            if not (type(u) is int and u < 2):
                wait(sp, s["kv_ps"], u - 1)
                wait(sp, s["k96_ok"], u - 1)
                sp.nop().then_inc(s["waited"], 1)
            sp.dma_start(cT[b][:, :], io.cache_c[bass.ds(u, 1)].rearrange("a c n -> (a c) n")).then_inc(s[f"in{b}"], 16)
            sp.dma_start(krc[b][:, :], io.cache_kr[bass.ds(u, 1)].rearrange("a n d -> (a n) d")).then_inc(s[f"in{b}"], 16)

        step(0, 0, 0)
        step(1, 1, 0)
        with sp.Fori(1, CT // 2) as i:
            step(i * 2, 0, i)
            step(i * 2 + 1, 1, i)
        sp.wait_ge(s["osn_ok"], 2)
        for h in range(H):
            sp.dma_start(at_s[:, h * VD:(h + 1) * VD], osn[32 * (h % 4):32 * (h % 4) + 32, h // 4, :]).then_inc(s["at_in"], 16)

    @block.tensor
    def _(pe):
        def kv(u, b, i):
            pe.wait_ge(s[f"in{b}"], i * 32 + 32)
            if not (type(u) is int and u < 2):
                wait(pe, s["k96_ok"], u - 1)
                wait(pe, s["v_ok"], u * 2 - 2)
            for a in range(2):
                last = pe.matmul(pb[2 * b + a][:, :], cT[b][:, :], g.wkv[:, a * 512:(a + 1) * 512], start=True, stop=True)
            last.then_inc(s["kv_ps"], 1)

        def step(u, b, i):
            if not (type(u) is int and u == CT - 1):
                kv(u + 1, 1 - b, i + b)
            wait(pe, s["k96_ok"], u + 1)
            if not (type(u) is int and u == 0):
                wait(pe, s["kT_a"], u)
                wait(pe, s["kT_b"], u)
            for h in range(H):
                last = pe.transpose(pb[4 + h // 4][0:QKD, h % 4 * P:(h % 4 + 1) * P], k96[:, h, :], ident)
            last.then_inc(s["kT_ps"], 1)
            wait(pe, s["kT_a"], u + 1)
            wait(pe, s["kT_b"], u + 1)
            wait(pe, s["sc_ok"], u)
            for h in range(H):
                a = 32 * (h % 4)
                last = pe.matmul(pb[6][a:a + 32, h // 4 * P:(h // 4 + 1) * P], g.q_new[:, h, :], kTc[b][:, h, :], start=True, stop=True)
            last.then_inc(s["sc_ps"], 1)

        kv(0, 0, 0)
        cache_tiles(pe, step)
        for h in range(H):
            a = 32 * (h % 4)
            last = pe.matmul(pb[7][a:a + 32, h // 4 * SAMPLE:(h // 4 + 1) * SAMPLE], g.q_new[:, h, :], g.k_new[:, h, :], start=True, stop=True)
        last.then_inc(s["new_ps"], 1)
        n = 0
        for f in range(2):
            pe.wait_ge(s["p_ok"], f + 1)
            for a in range(0, CT + 1, 4):
                if n >= 2:
                    pe.wait_ge(s[f"ev{n % 2}"], n // 2)
                for x in range(a, min(a + 4, CT + 1)):
                    w = P if x < CT else SAMPLE
                    last = pe.transpose(pb[4 + n % 2][0:w, (x - a) * P:(x - a + 1) * P], sc[:, f, x * P:x * P + w], ident)
                last.then_inc(s["tr_ps"], 1)
                n += 1
            for k in (n - 2, n - 1):
                pe.wait_ge(s[f"ev{k % 2}"], k // 2 + 1)
            for h in range(4 * f, 4 * f + 4):
                a = 32 * (h % 4)
                for x in range(CT):
                    pe.matmul(pb[f][a:a + 32, 0:VD], pTc[:, x, a:a + 32], vc[:, x, h * VD:(h + 1) * VD], start=x == 0, stop=False)
                last = pe.matmul(pb[f][a:a + 32, 0:VD], pTc[0:SAMPLE, CT, a:a + 32], g.v_new[:, h, :], start=False, stop=True)
            last.then_inc(s["o_ps"], 1)
        pe.wait_ge(s["as_ok"], 1)
        for j in range(4):
            last = pe.transpose(pb[6][:, j * SAMPLE:(j + 1) * SAMPLE], at_s[:, j * P:(j + 1) * P], ident[0:SAMPLE, 0:SAMPLE])
        last.then_inc(s["at_ps"], 1)

    def four(bank):
        return bank.rearrange("p (h n) -> p h n", h=4)

    @block.scalar
    def _(act):
        def step(u, b, i):
            wait(act, s["kv_ps"], u + 1)
            if not (type(u) is int and u == 0):
                wait(act, s["red_ok"], u)
            for a in range(2):
                act.activation(sq[:, 4 * a:4 * a + 4, :], four(pb[2 * b + a][:, :])[:, :, 0:NOPE], ACT.Square).then_inc(s["sq_ok"], 1)
            for a in range(2):
                act.activation(vc[:, bass.ds(u, 1), 256 * a:256 * a + 256].rearrange("p u (h n) -> p (u h) n", h=4),
                               four(pb[2 * b + a][:, :])[:, :, NOPE:], ACT.Copy).then_inc(s["v_ok"], 1)
            wait(act, s["kT_ps"], u + 1)
            act.activation(kTc[b][:, 0:4, :], pb[4][0:QKD, :].rearrange("p (h n) -> p h n", h=4), ACT.Copy).then_inc(s["kT_a"], 1)

        cache_tiles(act, step)
        for f in range(2):
            act.wait_ge(s["top_ok"], 1)
            act.activation(sc[:, f, :], sc[:, f, :], ACT.Exp, bias=top[:, f:f + 1], scale=ATTN_SCALE,
                           accum_out=total[:, f:f + 1]).then_inc(s["p_ok"], 1)
        act.wait_ge(s["at_in"], 16 * H)
        act.activation(junk[:, :], at_s[:, :], ACT.Square, accum_out=norm[:, 0:1]).then_inc(s["asq_ok"], 1)

    @block.gpsimd
    def _(pool):
        def step(u, b, i):
            wait(pool, s["ms_ok"], u + 1)
            pool.tensor_tensor(r8[:, :], r8[:, :], minus_half, ALU.pow).then_inc(s["r_ok"], 1)

        cache_tiles(pool, step)
        pool.wait_ge(s["am_ok"], 1)
        pool.tensor_tensor(norm[:, :], norm[:, :], minus_half[0:SAMPLE, 0:1], ALU.pow).then_inc(s["ar_ok"], 1)

    @block.vector
    def _(dve):
        def step(u, b, i):
            wait(dve, s["sq_ok"], u * 2 + 2)
            dve.tensor_reduce(r8[:, :], sq[:, :, :], AX.X, ALU.add).then_inc(s["red_ok"], 1)
            wait(dve, s["red_ok"], u + 1)
            dve.tensor_scalar(r8[:, :], r8[:, :], 1.0 / NOPE, EPS, ALU.mult, ALU.add).then_inc(s["ms_ok"], 1)
            wait(dve, s["kT_ps"], u)
            dve.tensor_copy(k96[:, :, NOPE:], bcast(krc[b][:, :], 1, H)).then_inc(s["k_a"], 1)
            wait(dve, s["v_ok"], u * 2 + 2)
            wait(dve, s["r_ok"], u + 1)
            dve.tensor_tensor(k96[:, 0:4, 0:NOPE], four(pb[2 * b][:, :])[:, :, 0:NOPE], bcast(r8[:, 0:4], 2, NOPE), ALU.mult
                              ).then_inc(s["k_b"], 1)
            dve.tensor_tensor(k96[:, 4:8, 0:NOPE], four(pb[2 * b + 1][:, :])[:, :, 0:NOPE], bcast(r8[:, 4:8], 2, NOPE), ALU.mult
                              ).then_inc(s["k96_ok"], 1)
            wait(dve, s["kT_ps"], u + 1)
            dve.tensor_copy(kTc[b][:, 4:8, :], pb[5][0:QKD, :].rearrange("p (h n) -> p h n", h=4)).then_inc(s["kT_b"], 1)
            wait(dve, s["sc_ps"], u + 1)
            dve.tensor_copy(sc[:, :, bass.ds(u * P, P)], pb[6][:, 0:2 * P].rearrange("p (f n) -> p f n", f=2)).then_inc(s["sc_ok"], 1)

        cache_tiles(dve, step)
        dve.wait_ge(s["new_ps"], 1)
        dve.tensor_copy(sc[:, :, PAST:], pb[7][:, 0:2 * SAMPLE].rearrange("p (f n) -> p f n", f=2)).then_inc(s["new_ok"], 1)
        dve.wait_ge(s["new_ok"], 1)
        dve.wait_ge(s["sc_ok"], CT)
        dve.tensor_reduce(top[:, :], sc[:, :, :], AX.X, ALU.max).then_inc(s["top1"], 1)
        dve.wait_ge(s["top1"], 1)
        dve.tensor_scalar(top[:, :], top[:, :], -ATTN_SCALE, None, ALU.mult).then_inc(s["top_ok"], 1)
        n = 0
        for f in range(2):
            for a in range(0, CT + 1, 4):
                dve.wait_ge(s["tr_ps"], n + 1)
                if f:
                    dve.wait_ge(s["o_ps"], 1)
                m = min(4, CT - a)
                if m:
                    ins = dve.tensor_copy(pTc[:, a:a + m, :], pb[4 + n % 2][:, 0:m * P].rearrange("p (x n) -> p x n", n=P))
                else:
                    ins = dve.tensor_copy(pTc[0:SAMPLE, CT, :], pb[4 + n % 2][0:SAMPLE, 0:P])
                ins.then_inc(s[f"ev{n % 2}"], 1)
                n += 1
        dve.wait_ge(s["p_ok"], 2)
        dve.reciprocal(total[:, :], total[:, :]).then_inc(s["l_ok"], 1)
        dve.wait_ge(s["l_ok"], 1)
        for f in range(2):
            dve.wait_ge(s["o_ps"], f + 1)
            dve.tensor_scalar(osn[:, f, :], pb[f][:, 0:VD], total[:, f:f + 1], None, ALU.mult).then_inc(s["osn_ok"], 1)
        dve.wait_ge(s["asq_ok"], 1)
        dve.tensor_scalar(norm[:, :], norm[:, :], 1.0 / MLA_OUT, EPS, ALU.mult, ALU.add).then_inc(s["am_ok"], 1)
        dve.wait_ge(s["ar_ok"], 1)
        dve.tensor_scalar(at_s[:, :], at_s[:, :], norm[:, 0:1], None, ALU.mult).then_inc(s["as_ok"], 1)
        dve.wait_ge(s["at_ps"], 1)
        dve.wait_ge(s["g_in"], 16)
        dve.tensor_tensor(g.mixT[:, 0:4, SEQ:], pb[6][:, 0:P].rearrange("p (j n) -> p j n", j=4),
                          bcast(g_attn[:, :], 2, SAMPLE), ALU.mult).then_inc(s["at_ok"], 1)


def output_projection(nc, g, io, phase):
    sb, sem, pb, con = phase.sb, g.sem, g.pb, g.con
    wo = [sb(f"wo{i}", [P, KD, P]) for i in range(2)]
    hsq = sb("hsq", [P, TOK])
    acc = sb("acc", [P, TOK])
    ones = sb("ones", [P, P])
    TT_ = -(-TOK // P)
    width = [min(P, TOK - P * t) for t in range(TT_)]
    row_ms = sb("row_ms", [P, TT_])
    diag = sb("diag", [P, TT_, P])
    ident = con[:, CON["ident"][0]:CON["ident"][0] + P]
    minus_half = con[:, CON["minus_half"][0]:CON["minus_half"][0] + TT_]
    g_ffn = sb("g_ffn", [P, KD])
    s = {n: sem("o_" + n) for n in """x_in in0 in1 waited zero ps_done h_ok sq_ok acc_ok ssq_ps ms_ok r_ok diag_ok rb_ps rb_ok u_ok""".split()}
    block = phase.block()

    @block.sync
    def _(sp):
        def load(u, b):
            sp.dma_start(wo[b][:, :, :], io.w_out[bass.ds(u, 1)].rearrange("a p k n -> (a p) k n")).then_inc(s[f"in{b}"], 16)

        load(0, 0)
        load(1, 1)
        sp.dma_start(g.hT[:, :, :], io.x_cols.rearrange("k p n -> p k n")).then_inc(s["x_in"], 16)
        sp.dma_start(g_ffn[:, :], io.g_ffn).then_inc(s["x_in"], 16)
        with sp.Fori(1, KD // 2) as i:
            for b in range(2):
                sp.wait_ge(s["ps_done"], i * 6 - 3 * (2 - b) + 3)
                sp.nop().then_inc(s["waited"], 1)
                load(i * 2 + b, b)
        sp.wait_ge(s["x_in"], 32)

    @block.tensor
    def _(pe):
        with pe.Fori(0, KD // 2) as i:
            for b in range(2):
                pe.wait_ge(s[f"in{b}"], i * 16 + 16)
                for n in range(3):
                    pe.wait_ge(s["h_ok"], i * 6 + 3 * b + n + 1)
                    for k in range(KD):
                        last = pe.matmul(pb[3 * b + n][:, 0:TN], wo[b][:, k, :], g.mixT[:, k, n * TN:(n + 1) * TN],
                                         start=k == 0, stop=k == KD - 1)
                    last.then_inc(s["ps_done"], 1)
        pe.wait_ge(s["acc_ok"], KD)
        pe.wait_ge(s["h_ok"], 3 * KD + 6)
        for t, w in enumerate(width):
            last = pe.matmul(pb[6][0:w, t:t + 1], acc[:, t * P:t * P + w], ones[:, 0:1], start=True, stop=True)
        last.then_inc(s["ssq_ps"], 1)
        pe.wait_ge(s["diag_ok"], TT_)
        for t, w in enumerate(width):
            last = pe.matmul(pb[t // 4][:, t % 4 * P:t % 4 * P + w], ones[0:w, :], diag[0:w, t, 0:w], start=True, stop=True)
        last.then_inc(s["rb_ps"], 1)

    @block.gpsimd
    def _(pool):
        pool.wait_ge(s["ms_ok"], 2)
        pool.tensor_tensor(row_ms[:, :], row_ms[:, :], minus_half, ALU.pow).then_inc(s["r_ok"], 1)

    @block.vector
    def _(dve):
        credit(dve, s["h_ok"], 6)
        dve.memset(acc[:, :], 0.0).then_inc(s["zero"], 1)
        dve.memset(ones[:, :], 1.0).then_inc(s["zero"], 1)
        dve.memset(row_ms[:, :], 1.0).then_inc(s["zero"], 1)
        dve.wait_ge(s["zero"], 3)
        dve.wait_ge(s["x_in"], 32)
        with dve.Fori(0, KD // 2) as i:
            for b in range(2):
                u = i * 2 + b
                for n in range(3):
                    c = slice(n * TN, (n + 1) * TN)
                    dve.wait_ge(s["ps_done"], u * 3 + n + 1)
                    h = g.hT[:, bass.ds(u, 1), c].rearrange("p a n -> p (a n)")
                    dve.tensor_tensor(h, pb[3 * b + n][:, 0:TN], h, ALU.add).then_inc(s["h_ok"], 1)
                dve.wait_ge(s["h_ok"], u * 3 + 9)
                h = g.hT[:, bass.ds(u, 1), :].rearrange("p a n -> p (a n)")
                dve.tensor_tensor(hsq[:, :], h, h, ALU.mult).then_inc(s["sq_ok"], 1)
                dve.wait_ge(s["sq_ok"], u + 1)
                dve.tensor_tensor(acc[:, :], acc[:, :], hsq[:, :], ALU.add).then_inc(s["acc_ok"], 1)
                dve.wait_ge(s["acc_ok"], u + 1)
        dve.wait_ge(s["ssq_ps"], 1)
        full = TOK // P
        dve.tensor_scalar(row_ms[:, 0:full], pb[6][:, 0:full], 1.0 / D, EPS, ALU.mult, ALU.add).then_inc(s["ms_ok"], 1)
        dve.tensor_scalar(row_ms[0:width[-1], full:], pb[6][0:width[-1], full:TT_], 1.0 / D, EPS, ALU.mult, ALU.add
                          ).then_inc(s["ms_ok"], 1)
        dve.wait_ge(s["r_ok"], 1)
        for t in range(TT_):
            dve.tensor_scalar(diag[:, t, :], ident, row_ms[:, t:t + 1], None, ALU.mult).then_inc(s["diag_ok"], 1)
        dve.wait_ge(s["rb_ps"], 1)
        for n in range(0, TOK, 512):
            w = min(512, TOK - n)
            dve.tensor_copy(acc[:, n:n + w], pb[n // 512][:, 0:w]).then_inc(s["rb_ok"], 1)
        dve.wait_ge(s["rb_ok"], 3)
        for k in range(KD):
            dve.scalar_tensor_tensor(g.mixT[:, k, :], g.hT[:, k, :], g_ffn[:, k:k + 1], acc[:, :], ALU.mult, ALU.mult
                                     ).then_inc(s["u_ok"], 1)


def ffn_up(nc, g, io, phase):
    sb, sem, pb = phase.sb, g.sem, g.pb
    wg = [sb(f"wg{i}", [P, KD, P]) for i in range(2)]
    wu = [sb(f"wu{i}", [P, KD, P]) for i in range(2)]
    th = [sb(f"th{i}", [P, TN]) for i in range(3)]
    s = {n: sem("u_" + n) for n in "in0 in1 waited g_ps u_ps th_ok t_ok hid_ok".split()}
    block = phase.block()

    @block.sync
    def _(sp):
        def load(u, b):
            sp.dma_start(wg[b][:, :, :], io.w_gate[bass.ds(u, 1)].rearrange("a p k n -> (a p) k n")).then_inc(s[f"in{b}"], 16)
            sp.dma_start(wu[b][:, :, :], io.w_up[bass.ds(u, 1)].rearrange("a p k n -> (a p) k n")).then_inc(s[f"in{b}"], 16)

        load(0, 0)
        load(1, 1)
        with sp.Fori(1, FB // 2) as i:
            for b in range(2):
                sp.wait_ge(s["u_ps"], i * 6 - 6 + 3 * (b + 1))
                sp.nop().then_inc(s["waited"], 1)
                load(i * 2 + b, b)

    @block.tensor
    def _(pe):
        with pe.Fori(0, FB // 2) as i:
            for b in range(2):
                pe.wait_ge(s[f"in{b}"], i * 32 + 32)
                for n in range(3):
                    m = 3 * b + n
                    pe.wait_ge(s["hid_ok"], i * 6 + m + 1)
                    for w, bank, done in ((wg, n, "g_ps"), (wu, 3 + n, "u_ps")):
                        for k in range(KD):
                            last = pe.matmul(pb[bank][:, 0:TN], w[b][:, k, :], g.mixT[:, k, n * TN:(n + 1) * TN],
                                             start=k == 0, stop=k == KD - 1)
                        last.then_inc(s[done], 1)

    @block.scalar
    def _(act):
        with act.Fori(0, FB // 2) as i:
            for b in range(2):
                for n in range(3):
                    m = 3 * b + n
                    act.wait_ge(s["g_ps"], i * 6 + m + 1)
                    act.activation(th[n][:, :], pb[n][:, 0:TN], ACT.Tanh, scale=0.5).then_inc(s["th_ok"], 1)

    @block.vector
    def _(dve):
        credit(dve, s["hid_ok"], 3)
        with dve.Fori(0, FB // 2) as i:
            for b in range(2):
                for n in range(3):
                    m = 3 * b + n
                    dve.wait_ge(s["th_ok"], i * 6 + m + 1)
                    dve.scalar_tensor_tensor(th[n][:, :], th[n][:, :], 1.0, pb[n][:, 0:TN], ALU.add, ALU.mult).then_inc(s["t_ok"], 1)
                    dve.wait_ge(s["t_ok"], i * 6 + m + 1)
                    dve.wait_ge(s["u_ps"], i * 6 + m + 1)
                    dve.scalar_tensor_tensor(g.hid[:, bass.ds(i * 2 + b, 1), n * TN:(n + 1) * TN].rearrange("p a n -> p (a n)"),
                                             th[n][:, :], 0.5, pb[3 + n][:, 0:TN], ALU.mult, ALU.mult).then_inc(s["hid_ok"], 1)


def ffn_down(nc, g, io, phase):
    sb, sem, pb = phase.sb, g.sem, g.pb
    wd = [sb(f"wd{i}", [P, FB, P]) for i in range(2)]
    y = [g.mixT[:, i, :] for i in range(2)]
    s = {n: sem("d_" + n) for n in "in0 in1 waited ps_done y_ok y_out0 y_out1".split()}
    block = phase.block()

    @block.sync
    def _(sp):
        def load(u, b):
            sp.dma_start(wd[b][:, :, :], io.w_down[bass.ds(u, 1)].rearrange("a p k n -> (a p) k n")).then_inc(s[f"in{b}"], 16)

        load(0, 0)
        load(1, 1)
        for b in range(2):
            credit(sp, s[f"y_out{b}"], 1)

        def store(i, b):
            sp.wait_ge(s["y_ok"], i * 6 + 3 * (b + 1) + 6)
            sp.nop().then_inc(s["waited"], 1)
            sp.dma_start(io.y[bass.ds(i * 2 + b, 1)].rearrange("a p n -> (a p) n"), y[b]).then_inc(s[f"y_out{b}"], 16)

        with sp.Fori(0, KD // 2 - 1) as i:
            for b in range(2):
                store(i, b)
                load(i * 2 + 2 + b, b)
        for b in range(2):
            store(KD // 2 - 1, b)
        for b in range(2):
            sp.wait_ge(s[f"y_out{b}"], 8 * KD + 1)

    @block.tensor
    def _(pe):
        with pe.Fori(0, KD // 2) as i:
            for b in range(2):
                pe.wait_ge(s[f"in{b}"], i * 16 + 16)
                for n in range(3):
                    pe.wait_ge(s["y_ok"], i * 6 + 3 * b + n + 1)
                    for k in range(FB):
                        last = pe.matmul(pb[3 * b + n][:, 0:TN], wd[b][:, k, :], g.hid[:, k, n * TN:(n + 1) * TN],
                                         start=k == 0, stop=k == FB - 1)
                    last.then_inc(s["ps_done"], 1)

    @block.vector
    def _(dve):
        credit(dve, s["y_ok"], 6)
        with dve.Fori(0, KD // 2) as i:
            for b in range(2):
                u = i * 2 + b
                dve.wait_ge(s[f"y_out{b}"], i * 16 + 1)
                for n in range(3):
                    c = slice(n * TN, (n + 1) * TN)
                    dve.wait_ge(s["ps_done"], u * 3 + n + 1)
                    dve.tensor_tensor(y[b][:, c], pb[3 * b + n][:, 0:TN],
                                      g.hT[:, bass.ds(u, 1), c].rearrange("p a n -> p (a n)"), ALU.add).then_inc(s["y_ok"], 1)


class Phase:

    def __init__(self, nc):
        self.nc, self.ctx = nc, ExitStack()

    def __enter__(self):
        return self

    def __exit__(self, *a):
        return self.ctx.__exit__(*a)

    def sb(self, name, shape):
        return self.ctx.enter_context(self.nc.sbuf_tensor(name, shape, F32))

    def block(self):
        return self.ctx.enter_context(self.nc.Block())


class Shared:
    pass


def nc_bank_run(g, first, n):
    return g.psum[:, 512 * first:512 * (first + n)]


def hybrid_layer(nc, io):
    with ExitStack() as ctx:
        g = Shared()
        taken = []

        def take(name):
            taken.append(nc.alloc_semaphore(name=name))
            return taken[-1]

        g.sem = take
        psum = ctx.enter_context(nc.psum_tensor("psum", [P, 8 * 512], F32))
        g.psum = psum
        g.pb = [psum[:, 512 * i:512 * (i + 1)] for i in range(8)]
        g.con = ctx.enter_context(nc.sbuf_tensor("con", [P, CONS], F32))
        with Phase(nc) as early:
            g.wkv = early.sb("wkv", [P, H * (NOPE + VD)])
            g.k_new = early.sb("k_new", [QKD, H, SAMPLE])
            g.q_new = early.sb("q_new", [QKD, H, SAMPLE])
            g.v_new = early.sb("v_new", [SAMPLE, H, VD])
            with Phase(nc) as phase:
                layer_inputs(nc, g, io, phase)
            nc.clear_and_free_semaphores(taken)
            nc.all_engine_barrier()
            g.mixT = early.sb("mixT", [P, KD, TOK])
            g.hT = early.sb("hT", [P, KD, TOK])
            for part in (prompt_attention, sample_attention, output_projection):
                with Phase(nc) as phase:
                    part(nc, g, io, phase)
            g.hid = early.sb("hid", [P, FB, TOK])
            for part in (ffn_up, ffn_down):
                with Phase(nc) as phase:
                    part(nc, g, io, phase)


def kernel(**inputs):
    import concourse.bacc as _bacc
    from concourse.bass_utils import run_bass_kernel_spmd as _run

    a = {n: np.asarray(v) for n, v in inputs.items()}
    T = np.ascontiguousarray
    rows = np.zeros((TILES * P, D), np.float32)
    rows[0:META] = a["meta_tokens"]
    rows[SAMPLE_ROW:SAMPLE_ROW + SAMPLE] = a["x_sample"][0]
    rows[P:] = a["x_prompt"][0]
    pairs = np.zeros((P, 4, P), np.float32)
    for h in range(H):
        r = slice(CHUNK * (h % 2), CHUNK * (h % 2) + CHUNK)
        pairs[r, h // 2, r] = a["state_wkv"][0, h].T
    ext = {
        "x_tiles": T(rows.reshape(TILES, P, KD, P).transpose(0, 3, 2, 1)),
        "x_cols": T(np.concatenate([a["x_prompt"][0], a["x_sample"][0]]).T.reshape(KD, P, TOK)),
        "w_in": T(a["w_in"].reshape(KD, P, IPC, IPW).transpose(2, 1, 0, 3)),
        "g_mix": T(a["norm_mix_g"].reshape(KD, P).T),
        "con": constants(),
        "vec": np.concatenate([a[n].reshape(-1) for n in VEC]),
        "w_q_up": T(a["w_q_up"].reshape(QL // P, P, H * QKD).transpose(1, 0, 2)),
        "w_kv_up": a["w_kv_up"],
        "w2a2": np.concatenate([a["w2"], a["a2"]]),
        "g2": a["g2"],
        "state_wkv": pairs,
        "state_shift": a["state_shift"],
        "cache_c": T(a["cache_kv_latent"][0].reshape(PAST // P, P, KVL).transpose(0, 2, 1)),
        "cache_kr": a["cache_k_rope"][0].reshape(PAST // P, P, ROPE),
        "g_attn": T(a["attn_out_g"].reshape(4, P).T),
        "g_ffn": T(a["norm_ffn_g"].reshape(KD, P).T),
        "w_out": T(a["w_out"].reshape(KD, P, KD, P).transpose(2, 1, 0, 3)),
        "w_gate": T(a["w_gate"].reshape(KD, P, FB, P).transpose(2, 1, 0, 3)),
        "w_up": T(a["w_up"].reshape(KD, P, FB, P).transpose(2, 1, 0, 3)),
        "w_down": T(a["w_down"].reshape(FB, P, KD, P).transpose(2, 1, 0, 3)),
    }
    outs = {
        "y": (KD, P, TOK), "c_p": (KEYS, KVL), "kr_p": (KEYS, ROPE), "wkv_p": (P, 4, CHUNK), "shift_p": (1, RCOLS),
        "c_s": (SAMPLE, KVL), "kr_s": (SAMPLE, ROPE), "wkv_s": (P, 4, CHUNK), "shift_s": (1, RCOLS),
    }
    scratch = {"kT": (H, QKD, KEYS), "qT": (H, QKD, SEQ), "v": (TILES, P, H, VD), "rwT": (4, P, TILES * P)}
    nc = _bacc.Bacc("TRN2", target_bir_lowering=False, num_devices=1)
    io = Shared()
    arrays = {}
    io.x_tiles = None
    handles = {}
    for n, v in ext.items():
        arrays["in_" + n] = v
        handles[n] = nc.dram_tensor("in_" + n, v.shape, F32, kind="ExternalInput").ap()
    for n, v in outs.items():
        handles[n] = nc.dram_tensor("out_" + n, v, F32, kind="ExternalOutput").ap()
    for n, v in scratch.items():
        handles[n] = nc.dram_tensor("scratch_" + n, v, F32, kind="Internal").ap()
    handles["kT"] = handles["kT"].rearrange("h d n -> d h n")
    handles["qT"] = handles["qT"].rearrange("h d n -> d h n")
    handles["rwT"] = handles["rwT"].rearrange("j p n -> p j n")
    vars(io).update(handles)
    hybrid_layer(nc, io)
    r = _run(nc, [arrays], core_ids=[0]).results[0]

    def state(x):
        return T(x.reshape(2, CHUNK, 4, CHUNK).transpose(2, 0, 3, 1).reshape(1, H, CHUNK, CHUNK))

    y = r["out_y"].reshape(D, TOK).T
    return (T(y[None, :SEQ]), T(y[None, SEQ:]), r["out_c_p"][None], r["out_kr_p"][None], state(r["out_wkv_p"]),
            r["out_shift_p"], r["out_c_s"][None], r["out_kr_s"][None], state(r["out_wkv_s"]), r["out_shift_s"])
```
